# Optimizing a Trainium2 kernel written in Bass

```python
import math
import jax, jax.numpy as jnp
from jax import lax
import numpy as np

D_MODEL = 1024
BATCH = 1
SEQ = 256
DEPTH = 1

N_BRANCH = 4
BRANCH_W = D_MODEL // 4
POOL_WINDOWS = (2, 4, 8, 16)
POOL_GROUPS = len(POOL_WINDOWS)
POOL_GW = BRANCH_W // POOL_GROUPS
SG_HEADS = 4
SG_CHUNK = 128
SG_HD = BRANCH_W // SG_HEADS
CONV_WIDTH = 31
ATT_HEADS = 4
ATT_HD = BRANCH_W // ATT_HEADS
ATT_BLOCK = 128
COL_SIZES = (
    BRANCH_W,
    2 * BRANCH_W,
    2 * BRANCH_W,
    BRANCH_W,
    BRANCH_W,
    BRANCH_W,
    ATT_HEADS,
    N_BRANCH * D_MODEL,
)
COL_TOTAL = int(sum(COL_SIZES))
COL_SPLITS = tuple(int(i) for i in np.cumsum(COL_SIZES)[:-1])
N_EXPERTS = 64
TOP_K = 6
N_GROUPS = 8
TOPK_GROUPS = 4
EXPERT_FF = 256
SHARED_FF = 256
ROUTE_SCALE = 2.5
MOE_CHUNK = 128
EPS = 1e-6
N_MOD = 6

kernel_name = "hybrid_pool_sgmlp_conformer_fox_moe_adaln"

def rms_norm(x, g):
    x32 = x.astype(jnp.float32)
    y = x32 * lax.rsqrt(jnp.mean(x32 * x32, axis=-1, keepdims=True) + EPS)
    return (y * g.astype(jnp.float32)).astype(x.dtype)

def layer_norm(x, g, b):
    x32 = x.astype(jnp.float32)
    mu = jnp.mean(x32, axis=-1, keepdims=True)
    var = jnp.mean(jnp.square(x32 - mu), axis=-1, keepdims=True)
    y = (x32 - mu) * lax.rsqrt(var + EPS)
    return (y * g.astype(jnp.float32) + b.astype(jnp.float32)).astype(x.dtype)

def multiscale_pool(u, w_pool, scale):
    B, S, _ = u.shape
    ug = u.reshape(B, S, POOL_GROUPS, POOL_GW).astype(jnp.float32)
    cs = jnp.cumsum(ug, axis=1)
    count = jnp.arange(1, S + 1, dtype=jnp.float32)
    outs = []
    for gi, w in enumerate(POOL_WINDOWS):
        csg = cs[:, :, gi]
        lag = jnp.pad(csg, ((0, 0), (w, 0), (0, 0)))[:, :S]
        mean = (csg - lag) / jnp.minimum(count, float(w))[None, :, None]
        outs.append(mean - ug[:, :, gi])
    pooled = jnp.stack(outs, axis=2)
    y = jnp.einsum('bsgc,gcd->bsgd', pooled, w_pool.astype(jnp.float32)).reshape(B, S, BRANCH_W)
    return (y * scale.astype(jnp.float32)).astype(u.dtype)

def spatial_gating(z, ln_g, ln_b, w_s, b_s):
    B, S, _ = z.shape
    z = jax.nn.gelu(z)
    u, v = jnp.split(z, 2, axis=-1)
    v = layer_norm(v, ln_g, ln_b)
    vb = v.reshape(B, S // SG_CHUNK, SG_CHUNK, SG_HEADS, SG_HD)
    causal = jnp.tril(jnp.ones((SG_CHUNK, SG_CHUNK), dtype=w_s.dtype))
    s = jnp.einsum('hts,bnshc->bnthc', w_s * causal, vb)
    s = s + jnp.transpose(b_s)[None, None, :, :, None]
    return u * s.reshape(B, S, BRANCH_W)

def conformer_conv(z, conv_w, conv_b, ln_g, ln_b):
    a, g = jnp.split(z, 2, axis=-1)
    y = a * jax.nn.sigmoid(g)
    y = lax.conv_general_dilated(
        y, conv_w[:, None, :].astype(y.dtype), window_strides=(1,),
        padding=[(CONV_WIDTH - 1, 0)], dimension_numbers=('NWC', 'WIO', 'NWC'),
        feature_group_count=BRANCH_W) + conv_b
    y = layer_norm(y, ln_g, ln_b)
    return jax.nn.silu(y)

def forgetting_attention(q, k, v, f_logit):
    B, S, H, dh = q.shape
    nb = S // ATT_BLOCK
    log_f = jax.nn.log_sigmoid(f_logit.astype(jnp.float32))
    cum = jnp.cumsum(log_f, axis=1)
    cum_k = jnp.transpose(cum, (0, 2, 1))
    k32 = k.astype(jnp.float32)
    v32 = v.astype(jnp.float32)
    qb = jnp.transpose(q.reshape(B, nb, ATT_BLOCK, H, dh), (1, 0, 2, 3, 4))
    cb = jnp.transpose(cum.reshape(B, nb, ATT_BLOCK, H), (1, 0, 3, 2))
    starts = jnp.arange(nb, dtype=jnp.int32) * ATT_BLOCK
    kpos = jnp.arange(S, dtype=jnp.int32)
    scale = 1.0 / math.sqrt(dh)

    def one_block(args):
        q_blk, c_blk, start = args
        logits = jnp.einsum('bqhd,bkhd->bhqk', q_blk.astype(jnp.float32), k32) * scale
        logits = logits + c_blk[..., None] - cum_k[:, :, None, :]
        qpos = start + jnp.arange(ATT_BLOCK, dtype=jnp.int32)
        mask = kpos[None, :] <= qpos[:, None]
        logits = jnp.where(mask[None, None], logits, -jnp.inf)
        p = jax.nn.softmax(logits, axis=-1)
        return jnp.einsum('bhqk,bkhd->bqhd', p, v32)

    out = lax.map(one_block, (qb, cb, starts))
    out = jnp.transpose(out, (1, 0, 2, 3, 4)).reshape(B, S, H * dh)
    return out.astype(q.dtype)

def mixer_sublayer(h, w_in, b_f, pool_w, pool_scale, sg_ln_g, sg_ln_b, sg_w, sg_b,
                   conv_w, conv_b, conv_ln_g, conv_ln_b, w_branch, w_out):
    B, S, D = h.shape
    proj = jnp.einsum('bsd,dc->bsc', h, w_in)
    z_pool, z_sg, z_conv, q, k, v, f_logit, gate_cols = jnp.split(proj, COL_SPLITS, axis=-1)
    y_a = multiscale_pool(z_pool, pool_w, pool_scale)
    y_b = spatial_gating(z_sg, sg_ln_g, sg_ln_b, sg_w, sg_b)
    y_c = conformer_conv(z_conv, conv_w, conv_b, conv_ln_g, conv_ln_b)
    y_d = forgetting_attention(q.reshape(B, S, ATT_HEADS, ATT_HD),
                               k.reshape(B, S, ATT_HEADS, ATT_HD),
                               v.reshape(B, S, ATT_HEADS, ATT_HD),
                               f_logit + b_f)
    ys = jnp.stack([y_a, y_b, y_c, y_d.astype(y_a.dtype)], axis=2)
    branch = jnp.einsum('bsnc,ncd->bsnd', ys, w_branch)
    gates = jax.nn.sigmoid(gate_cols).reshape(B, S, N_BRANCH, D)
    merged = jnp.sum(gates * branch, axis=2)
    return jnp.einsum('bsd,de->bse', merged, w_out)

def moe_ffn(h, router_w, router_bias, w1, w3, w2, sw1, sw3, sw2):
    B, S, D = h.shape
    T = B * S
    t = h.reshape(T, D)
    scores = jax.nn.sigmoid(jnp.einsum('td,de->te', t, router_w).astype(jnp.float32))
    sel = scores + router_bias.astype(jnp.float32)
    grouped = sel.reshape(T, N_GROUPS, N_EXPERTS // N_GROUPS)
    group_score = jnp.sum(lax.top_k(grouped, 2)[0], axis=-1)
    _, gidx = lax.top_k(group_score, TOPK_GROUPS)
    gmask = jnp.sum(jax.nn.one_hot(gidx, N_GROUPS, dtype=jnp.float32), axis=1) > 0
    emask = jnp.repeat(gmask, N_EXPERTS // N_GROUPS, axis=1)
    _, eidx = lax.top_k(jnp.where(emask, sel, -jnp.inf), TOP_K)
    w = jnp.take_along_axis(scores, eidx, axis=1)
    w = w / jnp.sum(w, axis=-1, keepdims=True) * ROUTE_SCALE
    dense_gates = jnp.sum(jax.nn.one_hot(eidx, N_EXPERTS, dtype=jnp.float32) * w[..., None], axis=1)
    nchunk = T // MOE_CHUNK

    def chunk_fn(args):
        tc, gc = args
        a = jnp.einsum('td,edf->tef', tc, w1)
        b = jnp.einsum('td,edf->tef', tc, w3)
        hid = jax.nn.silu(a) * b * gc[:, :, None].astype(tc.dtype)
        return jnp.einsum('tef,efd->td', hid, w2)

    routed = lax.map(chunk_fn, (t.reshape(nchunk, MOE_CHUNK, D),
                                dense_gates.reshape(nchunk, MOE_CHUNK, N_EXPERTS))).reshape(T, D)
    shared = jnp.einsum('tf,fd->td', jax.nn.silu(t @ sw1) * (t @ sw3), sw2)
    return (routed + shared).reshape(B, S, D)

def setup_inputs(seed: int = 0) -> dict:
    key = jax.random.key(seed)
    ks = jax.random.split(key, 32)
    f32 = jnp.float32
    n = lambda i, shape: jax.random.normal(ks[i], shape, dtype=f32)
    L, D, E = DEPTH, D_MODEL, N_EXPERTS
    return {
        "x": n(0, (BATCH, SEQ, D)),
        "c": n(1, (BATCH, D)),
        "w_in": n(2, (L, D, COL_TOTAL)) * D ** -0.5,
        "b_f": 3.0 + 0.5 * n(3, (L, ATT_HEADS)),
        "pool_w": n(4, (L, POOL_GROUPS, POOL_GW, POOL_GW)) * POOL_GW ** -0.5,
        "pool_scale": 1.0 + 0.1 * n(5, (L, BRANCH_W)),
        "sg_ln_g": 1.0 + 0.1 * n(6, (L, BRANCH_W)),
        "sg_ln_b": 0.02 * n(7, (L, BRANCH_W)),
        "sg_w": n(8, (L, SG_HEADS, SG_CHUNK, SG_CHUNK)) * (0.5 * SG_CHUNK ** -0.5),
        "sg_b": 1.0 + 0.1 * n(9, (L, SG_HEADS, SG_CHUNK)),
        "conv_w": n(10, (L, CONV_WIDTH, BRANCH_W)) * CONV_WIDTH ** -0.5,
        "conv_b": 0.02 * n(11, (L, BRANCH_W)),
        "conv_ln_g": 1.0 + 0.1 * n(12, (L, BRANCH_W)),
        "conv_ln_b": 0.02 * n(13, (L, BRANCH_W)),
        "w_branch": n(14, (L, N_BRANCH, BRANCH_W, D)) * BRANCH_W ** -0.5,
        "w_out": n(15, (L, D, D)) * D ** -0.5,
        "mix_norm_g": 1.0 + 0.1 * n(16, (L, D)),
        "ffn_norm_g": 1.0 + 0.1 * n(17, (L, D)),
        "ada_w": n(18, (L, D, N_MOD * D)) * (0.5 * D ** -0.5),
        "ada_b": 0.02 * n(19, (L, N_MOD * D)),
        "router_w": n(20, (L, D, E)) * D ** -0.5,
        "router_bias": 0.01 * n(21, (L, E)),
        "exp_w1": n(22, (L, E, D, EXPERT_FF)) * D ** -0.5,
        "exp_w3": n(23, (L, E, D, EXPERT_FF)) * D ** -0.5,
        "exp_w2": n(24, (L, E, EXPERT_FF, D)) * EXPERT_FF ** -0.5,
        "shared_w1": n(25, (L, D, SHARED_FF)) * D ** -0.5,
        "shared_w3": n(26, (L, D, SHARED_FF)) * D ** -0.5,
        "shared_w2": n(27, (L, SHARED_FF, D)) * SHARED_FF ** -0.5,
        "final_norm_g": 1.0 + 0.1 * n(28, (D,)),
    }

def reference(x, c, w_in, b_f, pool_w, pool_scale, sg_ln_g, sg_ln_b, sg_w, sg_b,
              conv_w, conv_b, conv_ln_g, conv_ln_b, w_branch, w_out, mix_norm_g, ffn_norm_g,
              ada_w, ada_b, router_w, router_bias, exp_w1, exp_w3, exp_w2,
              shared_w1, shared_w3, shared_w2, final_norm_g):
    B = x.shape[0]
    c_act = jax.nn.silu(c)
    for l in range(DEPTH):
        mod = (c_act @ ada_w[l] + ada_b[l]).reshape(B, N_MOD, D_MODEL)
        shift_m, scale_m, gate_m = mod[:, 0, None], mod[:, 1, None], mod[:, 2, None]
        shift_f, scale_f, gate_f = mod[:, 3, None], mod[:, 4, None], mod[:, 5, None]
        h = rms_norm(x, mix_norm_g[l]) * (1.0 + scale_m) + shift_m
        mix = mixer_sublayer(h, w_in[l], b_f[l], pool_w[l], pool_scale[l], sg_ln_g[l], sg_ln_b[l],
                             sg_w[l], sg_b[l], conv_w[l], conv_b[l], conv_ln_g[l], conv_ln_b[l],
                             w_branch[l], w_out[l])
        x = x + gate_m * mix
        h = rms_norm(x, ffn_norm_g[l]) * (1.0 + scale_f) + shift_f
        ffn = moe_ffn(h, router_w[l], router_bias[l], exp_w1[l], exp_w3[l], exp_w2[l],
                      shared_w1[l], shared_w3[l], shared_w2[l])
        x = x + gate_f * ffn
    return rms_norm(x, final_norm_g)


_drawn_inputs = setup_inputs


def setup_inputs(seed=0):
    import zlib

    import numpy as np

    out = dict(_drawn_inputs(seed))
    spreads = {}
    factors = {'sg_ln_g': 3.095, 'sg_ln_b': 26.535, 'conv_b': 3.527, 'conv_ln_b': 3.761}
    for name, (base, spread) in spreads.items():
        noise = np.random.default_rng([zlib.crc32(name.encode()), seed]).standard_normal(out[name].shape)
        drawn = base * np.exp(spread * noise) if base else spread * noise
        out[name] = __import__('jax').numpy.asarray(drawn.astype(out[name].dtype))
    for name, factor in factors.items():
        out[name] = (out[name] * factor).astype(out[name].dtype)
    return out
```

```python
from contextlib import ExitStack

import concourse.bass as bass
from concourse import mybir

F32 = mybir.dt.float32
I32 = mybir.dt.int32
BF16 = mybir.dt.bfloat16
ALU = mybir.AluOpType
ACT = mybir.ActivationFunctionType
AX = mybir.AxisListType.X

P = 128
D = 1024
T = 256
TB = T // P
KD = D // P
BW = 256
NB = 4
HEADS = 4
HD = BW // HEADS
TAPS = 31
E = 64
TOPK = 6
GROUPS = 8
TOPG = 4
ROUTE_SCALE = 2.5
FF = 256
CAP = 64
PAIRS = E // 2
MAX_PASS = T // CAP
EPS = 1e-6
NEG = -1e30

COL = {"pool": 0, "sg_u": 256, "sg_v": 512, "conv_a": 768, "conv_g": 1024, "q": 1280, "k": 1536,
       "v": 1792, "f": 2048, "gate": 2052}

RING_PAIRS = 2
SLOTS = 6 * RING_PAIRS
UNIT = 2048
MIX = ["conv_g", "conv_a", "q", "k", "v", "sg_v", "sg_u", "pool"]
CONV_AT = 4
LAG = 3
N_GATE = 16


def unit_plan():
    units = [("ada", i) for i in range(8)] + [("mix", i) for i in range(8)]
    for g in range(N_GATE):
        if g % 4 == 3:
            units.append(("branch", g // 4))
        units += [("gate", g), ("ada", 8 + g)]
    units += [("out", i) for i in range(4)] + [("sw1", 0), ("sw3", 0), ("sw2", 0)]
    return units


UNITS = unit_plan()
SLOT = {u: i % SLOTS for i, u in enumerate(UNITS)}
BEFORE = {u: UNITS[i - SLOTS] for i, u in enumerate(UNITS) if i >= SLOTS}
FILLS = {u: i // SLOTS for i, u in enumerate(UNITS)}

CONST = {"ident": 128, "rows4": 128, "bias_sel": 24 * 32, "upper": 128, "strict": 128, "ones": 256,
         "mask": 384, "inv": 512, "iota": 64, "thr": 3}
C_AT, C_W = {}, 0
for _n, _w in CONST.items():
    C_AT[_n] = C_W
    C_W += _w
C_EARLY = C_AT["upper"]
PARAM = {"c": 8, "mix_g": 8, "pool_scale": 2, "conv_b": 2, "conv_g": 2, "conv_beta": 2,
         "conv_w": 2 * TAPS, "b_f": 1}
P_AT, P_W = {}, 0
for _n, _w in PARAM.items():
    P_AT[_n] = P_W
    P_W += _w
MISC = {"wf": KD * HEADS, "sg_w": HEADS * P, "pool_w": 2 * P, "sg_g": BW, "sg_beta": BW, "sg_bias": 2 * T}
M_AT, M_W = {}, 0
for _n, _w in MISC.items():
    M_AT[_n] = M_W
    M_W += _w
OUT_BANK = [6, 7, 4, 5]


def decoder_layer(nc, a, out):
    with ExitStack() as ctx:
        def sb(name, shape, dt=F32):
            return ctx.enter_context(nc.sbuf_tensor(name, shape, dt))

        def sem(name):
            return ctx.enter_context(nc.semaphore(name))

        def carver(region, size):
            at = [0]

            def carve(*shape, parts=P):
                n = 1
                for d in shape:
                    n *= d
                flat = region[0:parts, at[0]:at[0] + n]
                at[0] += n
                assert at[0] <= size, (at[0], size)
                if len(shape) == 1:
                    return flat
                names = "abcd"[:len(shape)]
                pattern = "p (" + " ".join(names) + ") -> p " + " ".join(names)
                return flat.rearrange(pattern, **{x: d for x, d in zip(names, shape)})
            return carve

        ring = sb("ring", [P, SLOTS, UNIT])
        const = sb("const", [P, C_W])
        par = sb("par", [P, P_W])
        misc = sb("misc", [P, M_W])
        x_sb = sb("x_sb", [P, TB, D])
        hT = sb("hT", [P, KD, T])
        router = sb("router", [P, KD, E])
        r_bias = sb("r_bias", [P, E])
        crep = sb("crep", [P, KD, 32])
        csig = sb("csig", [P, KD])
        cact = sb("cact", [P, KD])
        ada_b = sb("ada_b", [P, 256])
        part2 = sb("part2", [P, 2, 512])
        a_c = sb("a_c", [P, KD])
        s_c = sb("s_c", [P, KD])
        ssq = sb("ssq", [P, 8])
        rstd = sb("rstd", [P, 16])
        nmax = sb("nmax", [P, HEADS, 2])
        psum_p = sb("psum_p", [P, HEADS, 2])
        rden = sb("rden", [P, HEADS, 2])
        stats = sb("stats", [P, TB, 6])
        mv = sb("mv", [P, TB, 2])
        need = sb("need", [P, TB])
        wsum = sb("wsum", [P, TB])
        most = sb("most", [P, 1])
        over = sb("over", [P, 3])
        n_pass = sb("n_pass", [P, 1], I32)
        top8 = sb("top8", [P, TB, 8])

        def mi(name, pattern, **kw):
            return misc[:, M_AT[name]:M_AT[name] + MISC[name]].rearrange(pattern, **kw)

        wf = mi("wf", "p (k h) -> p k h", h=HEADS)
        sgw = mi("sg_w", "p (h t) -> p h t", h=HEADS)
        sg_g = misc[:, M_AT["sg_g"]:M_AT["sg_g"] + BW]
        sg_beta = misc[:, M_AT["sg_beta"]:M_AT["sg_beta"] + BW]
        sg_bias = mi("sg_bias", "p (j t) -> p j t", j=2)
        pool_w = mi("pool_w", "p (j d) -> p j d", j=2)

        PAD = TAPS - 1
        PP = 16
        KA = HD + 2
        reg1 = sb("reg1", [P, 2 * D])
        xn = reg1[:, :].rearrange("p (b d) -> p b d", b=TB)
        qa = reg1[0:KA, 0:D].rearrange("p (h t) -> p h t", h=HEADS)
        ka = reg1[0:KA, D:2 * D].rearrange("p (h t) -> p h t", h=HEADS)
        merged = reg1[:, :].rearrange("p (k t) -> p k t", k=KD)
        reg2 = sb("reg2", [P, 2 * D])
        part = reg2[:, :].rearrange("p (v d) -> p v d", v=2)
        probT = reg2[:, 0:HEADS * 384].rearrange("p (h t) -> p h t", h=HEADS)
        h2 = reg2[:, :].rearrange("p (b d) -> p b d", b=TB)
        reg3 = sb("reg3", [P, 2 * D])
        c3 = carver(reg3, 2 * D)
        zv, tv, zu, tu = c3(TB, BW), c3(TB, BW), c3(2, T), c3(2, T)
        gate_m, scale_f = reg3[:, 0:D], reg3[:, D:2 * D]
        final_g = scale_f
        reg4 = sb("reg4", [P, 2 * D])
        prob = reg4[:, 0:HEADS * 384].rearrange("p (h t) -> p h t", h=HEADS)
        gate_f, shift_f = reg4[:, 0:D], reg4[:, D:2 * D]
        W5 = 5 * (PP + T)
        reg5 = sb("reg5", [P, W5])
        junk = reg5[:, 0:D]
        c5 = carver(reg5, W5)
        w2s, w4s, w8s = c5(2, PP + T), c5(2, PP + T), c5(PP + T)
        W6 = 8284
        reg6 = sb("reg6", [P, W6])
        c6 = carver(reg6, W6)
        y = c6(NB, 2, T)
        gb = c6(2 * T)
        glu = c6(2, PAD + T)
        conv = c6(2, T)
        sq_c = c6(2, T)
        sig_c = c6(2, T)
        mean_c, rs_c = sig_c[:, 0, :], sig_c[:, 1, :]
        zp = c6(2, PP + T)
        pooled = c6(2, T)
        sig = c6(LAG + 2, 2 * T)
        logit = sig[:, 0:2, 0:384]
        v_sb = sig[:, 2, :].rearrange("p (b c) -> p b c", b=TB)
        fz = sig[0:HEADS, 3:5, :].rearrange("p a t -> p (a t)")[:, 0:3 * T].rearrange("p (r t) -> p r t", r=3)
        c6 = carver(reg6, W6)
        c6(NB * 2 * T + 2 * T)
        take = c6(TB * P).bitcast(BF16).rearrange("p (b t s) -> p b t s", b=2, t=TB)
        gtake = c6(2, TB, P)
        xg = c6(2, KD, P)
        turned = c6(2, 4, P)
        y_sb = c6(D)
        c5 = carver(reg5, W5)
        sg1, th, hid = c5(FF), c5(FF), c5(FF)
        c6 = carver(reg6, NB * 2 * T)
        score, sel, gt = c6(TB, E), c6(TB, E), c6(TB, E)
        eq, pre, picked = c6(TB, E), c6(TB, E), c6(TB, E)
        top = c6(TB, GROUPS, 8)
        gs, gt_g, eq_g, pre_g = (c6(TB, GROUPS) for _ in range(4))
        EP = E + 4
        pos = c6(TB, EP)
        gates = c6(TB, EP)
        hid_s = c6(TB, FF)
        hT_flat = hT[:, :, :].rearrange("p k t -> p (k t)")
        parts = [r.bitcast(BF16).rearrange("p (b d) -> p b d", b=TB)
                 for r in (reg3[:, 0:D], reg4[:, D:2 * D], hT_flat[:, 0:D])]
        hidT_s = hT_flat[:, D:D + 2 * T].rearrange("p (b j t) -> p b j t", b=TB, j=2)

        bank = [ctx.enter_context(nc.psum_tensor(f"bank{i}", [P, 512], F32)) for i in range(8)]
        B_UNIT = [0, 1]
        B_ADA, B_CAST = 2, 3
        B_OUT = [0, 1, 2, 3]
        B_GATH, B_HID, B_Y = 4, 5, [6, 7]

        landed = [sem(f"landed{s}") for s in range(SLOTS)]
        w13_landed = [sem(f"w13_landed{r}") for r in range(RING_PAIRS)]
        w2_landed = [sem(f"w2_landed{r}") for r in range(RING_PAIRS)]
        w13_used = [sem(f"w13_used{r}") for r in range(RING_PAIRS)]
        w2_used = [sem(f"w2_used{r}") for r in range(RING_PAIRS)]
        names = """x_in const_in par_in ada_b_in misc_in late_in v_step a_step p_step
            final_in c_sig c_rep x_sq x_var x_rstd xn_done xT_done ada_done ada_read vec_done ac_done h_done
            unit_done f_done f_read exp_f cum_done cum_rows  conv_done
            q_done k_done tv_done sigv_done v_var v_rstd vn_done tu_done sigu_done
            sgw_done sg_done sg_y pooled_done pool_mm pool_y zero_done
            csum_done conv_c cvar_done conv_var conv_rstd conv_n conv_sig conv_y
            logits_done logit_done exp_done prob_done pT_done pT_read av_done av_y
            gb_done merged_done branch_done part2_done cast_done cast_read out_mm
            x2_done x2_sq x2_var x2_rstd h2_done h2T_done h2T_read
            part_done rest_done sc_mm score_done picked_done rank_done npass_done sh_done sh_sig sh_hid sh_T sh_TT
            take_raw take_built gathered gath_read sig1_done th_done hid_done turn_done turn_read
            y0_done y_read pos_next sum_done x3_done x3_sq x3_var x3_rstd fin_done stored""".split()
        S = {n: sem(n) for n in names}
        unit_read = [sem(f"unit_read{b}") for b in range(2)]

        def cn(name, lo=0, hi=None):
            at = C_AT[name]
            return const[:, at + lo:at + (CONST[name] if hi is None else hi)]

        def pr(name, lo=0, hi=None):
            at = P_AT[name]
            return par[:, at + lo:at + (PARAM[name] if hi is None else hi)]

        ident = cn("ident")

        def unit(u):
            return ring[:, SLOT[u], :]

        def linker(eng, s):
            count = [0]

            def link(ins):
                count[0] += 1
                ins.then_inc(s, 1)
                eng.wait_ge(s, count[0])
            return link

        def source(u):
            kind, i = u
            if kind == "ada":
                return a["ada_w"][0, :, i * 256:(i + 1) * 256].rearrange("(p k) n -> p k n", k=KD)
            if kind in ("mix", "gate"):
                c = COL[MIX[i]] if kind == "mix" else COL["gate"] + (i % 4) * D + (i // 4) * 256
                return a["w_in"][0, :, c:c + 256].rearrange("(p k) n -> p k n", k=KD)
            if kind == "branch":
                return a["w_branch"][0, :, :, i * 256:(i + 1) * 256].rearrange("n (j p) d -> p (n j) d", p=P)
            if kind == "out":
                return a["w_out"][0, i * 256:(i + 1) * 256, :].rearrange("(j p) d -> p j d", p=P)
            if kind == "sw2":
                return a["shared_w2"][0].rearrange("(p j) d -> p (j d)", j=2)
            return a["shared_" + kind[1:]][0].rearrange("(p k) f -> p (k f)", k=KD)

        def used_up(u):
            kind, i = u
            return {"ada": (S["ada_done"], i + 1), "mix": (S["unit_done"], i + 1), "gate": (S["unit_done"], 9 + i),
                    "branch": (S["branch_done"], 4 * i + 4), "out": (S["out_mm"], 4)}[kind]

        w13_src = [a[n][0].rearrange("e (p k) f -> e p (k f)", k=KD) for n in ("exp_w1", "exp_w3")]
        w2_src = a["exp_w2"][0].rearrange("e (p j) d -> e p (j d)", j=2)

        block = ctx.enter_context(nc.Block())

        @block.sync
        def _(sp):
            sp.dma_start(x_sb[:, :, :], a["x"][0].rearrange("(b p) d -> p b d", p=P)).then_inc(S["x_in"], 16)
            for u in UNITS:
                if u in BEFORE:
                    sp.wait_ge(*used_up(BEFORE[u]))
                src = source(u)
                dst = unit(u)
                if len(src.shape) == 3:
                    dst = dst.rearrange("p (k n) -> p k n", k=src.shape[1])
                sp.dma_start(dst, src).then_inc(landed[SLOT[u]], 16)
            sp.wait_ge(S["npass_done"], 1)
            passes = sp.value_load(n_pass[0:1, 0:1], min_val=1, max_val=MAX_PASS)
            with sp.Fori(0, passes) as ps:
                with sp.Fori(0, PAIRS // RING_PAIRS) as it:
                    for r in range(RING_PAIRS):
                        use = ps * (PAIRS // RING_PAIRS) + it
                        sp.wait_ge(w13_used[r], use + 1)
                        for e in range(2):
                            for w in range(2):
                                sp.dma_start(ring[:, 6 * r + 2 * e + w, :],
                                             w13_src[w][bass.ds(it * (2 * RING_PAIRS) + (2 * r + e), 1)]
                                             .rearrange("e p n -> (e p) n")).then_inc(w13_landed[r], 16)
                        sp.wait_ge(w2_used[r], use + 1)
                        for e in range(2):
                            sp.dma_start(ring[:, 6 * r + 4 + e, :],
                                         w2_src[bass.ds(it * (2 * RING_PAIRS) + (2 * r + e), 1)]
                                         .rearrange("e p n -> (e p) n")).then_inc(w2_landed[r], 16)
            for k in range(4):
                sp.wait_ge(S["fin_done"], k + 1)
                tb, hf = k // 2, k % 2
                sp.dma_start(out[0, tb * P:(tb + 1) * P, hf * 512:(hf + 1) * 512],
                             h2[:, tb, hf * 512:(hf + 1) * 512]).then_inc(S["stored"], 16)
            sp.wait_ge(S["stored"], 64)

        @block.gpsimd
        def _(pool):
            link = linker(pool, S["p_step"])
            pool.wait_ge(S["ada_done"], 4)
            pool.dma_start(misc[:, :], a["misc"]).then_inc(S["misc_in"], 16)
            pool.dma_start(const[:, C_EARLY:], a["const"][:, C_EARLY:]).then_inc(S["misc_in"], 16)
            pool.dma_start(router[:, :, :], a["router_w"][0].rearrange("(p k) e -> p k e", k=KD)).then_inc(S["late_in"], 16)
            pool.dma_start(r_bias[:, :], a["router_bias"][0:1, :].partition_broadcast(P)).then_inc(S["late_in"], 16)
            link(pool.memset(glu[:, :, 0:PAD], 0.0))

            def fill(t, value, count):
                pool.memset(t, value).then_inc(S["zero_done"], 1)
                pool.wait_ge(S["zero_done"], count)

            fill(zp[:, :, 0:PP], 0.0, 1)
            pool.wait_ge(S["x_rstd"], 1)
            fill(w2s[:, :, 0:PP], 0.0, 2)
            fill(w4s[:, :, 0:PP], 0.0, 3)
            fill(w8s[:, 0:PP], 0.0, 4)
            pool.wait_ge(S["xT_done"], 2 * KD)
            fill(qa[HD:KA, :, :], 1.0, 5)
            fill(ka[HD:KA, :, :], 1.0, 6)
            pool.wait_ge(S["sg_y"], 1)
            pool.dma_start(scale_f, a["ffn_norm_g"][0:1, :].partition_broadcast(P)).then_inc(S["late_in"], 16)
            pool.wait_ge(S["h2_done"], TB)
            pool.dma_start(final_g, a["final_norm_g"].rearrange("(o d) -> o d", o=1).partition_broadcast(P))\
                .then_inc(S["final_in"], 16)
            pool.wait_ge(S["h2T_done"], 4)
            for i in range(2):
                pool.wait_ge(S["part_done"], i + 1)
                pool.tensor_tensor(h2, h2, parts[i], ALU.subtract).then_inc(S["rest_done"], 1)

        @block.scalar
        def _(act):
            link = linker(act, S["a_step"])
            act.dma_start(par[:, :], a["par"]).then_inc(S["par_in"], 16)
            act.dma_start(const[:, 0:C_EARLY], a["const"][:, 0:C_EARLY]).then_inc(S["const_in"], 16)
            act.dma_start(ada_b[:, :], a["ada_bp"]).then_inc(S["ada_b_in"], 16)
            act.wait_ge(S["par_in"], 16)
            act.activation(csig[:, :], pr("c"), ACT.Sigmoid).then_inc(S["c_sig"], 1)
            act.wait_ge(S["x_in"], 16)
            for tb in range(TB):
                link(act.activation(junk[:, :], x_sb[:, tb, :], ACT.Square, accum_out=ssq[:, tb:tb + 1]))
            act.activation(ssq[:, 2:4], ssq[:, 0:2], ACT.Copy, scale=1.0 / D).then_inc(S["x_sq"], 1)
            act.wait_ge(S["x_var"], 1)
            act.activation(rstd[:, 2:4], rstd[:, 0:2], ACT.Sqrt).then_inc(S["x_rstd"], 1)
            for b in range(4):
                act.wait_ge(S["ada_done"], 2 * b + 2)
                act.activation(part[:, b // 2, (b % 2) * 512:(b % 2 + 1) * 512], bank[b][:, :], ACT.Copy)\
                   .then_inc(S["ada_read"], 1)
            act.wait_ge(S["xT_done"], 2 * KD)
            act.wait_ge(S["ac_done"], 2)
            for k in range(4, KD):
                act.activation(hT[:, k, :], bank[4 + k // 2][:, (k % 2) * 256:(k % 2 + 1) * 256], ACT.Identity,
                               bias=s_c[:, k:k + 1], scale=a_c[:, k:k + 1]).then_inc(S["h_done"], 1)

            def read_unit(i):
                act.wait_ge(S["unit_done"], i + 1)

            def ub(i):
                return bank[B_UNIT[i % 2]]

            read_unit(0)
            act.activation(sig_c[:, :, :].rearrange("p j t -> p (j t)"), ub(0)[:, :], ACT.Sigmoid)\
               .then_inc(unit_read[0], 1)
            act.wait_ge(S["f_read"], 2)
            link(act.activation(fz[:, 2, :], fz[:, 1, :], ACT.Exp, scale=-1.0))
            act.activation(fz[:, 1, :], fz[:, 2, :], ACT.Ln, bias=1.0).then_inc(S["exp_f"], 1)
            read_unit(2)
            act.wait_ge(S["zero_done"], 6)
            for h in range(HEADS):
                lo = 64 * (h % 2)
                ins = act.activation(qa[0:HD, h, :], ub(2)[lo:lo + HD, (h // 2) * T:(h // 2 + 1) * T], ACT.Copy,
                                     scale=HD ** -0.5)
                ins.then_inc(unit_read[0] if h == HEADS - 1 else S["q_done"], 1)
            read_unit(3)
            for h in range(HEADS):
                lo = 64 * (h % 2)
                ins = act.activation(ka[0:HD, h, :], ub(3)[lo:lo + HD, (h // 2) * T:(h // 2 + 1) * T], ACT.Copy)
                ins.then_inc(unit_read[1] if h == HEADS - 1 else S["k_done"], 1)
            act.wait_ge(S["cum_done"], 2)
            act.dma_start(qa[HD:HD + 1, :, :], fz[:, 0:1, :]).then_inc(S["cum_rows"], 16)
            act.dma_start(ka[HD + 1:HD + 2, :, :], fz[:, 1:2, :]).then_inc(S["cum_rows"], 16)
            read_unit(4)
            act.activation(v_sb[:, :, :].rearrange("p b c -> p (b c)"), ub(4)[:, :], ACT.Copy)\
               .then_inc(unit_read[0], 1)

            def exps(h):
                act.wait_ge(S["logit_done"], 3 * (h + 1))
                for qb in range(2):
                    lo, n = (0, P) if qb == 0 else (P, T)
                    act.activation(prob[:, h, lo:lo + n], logit[:, h % 2, lo:lo + n], ACT.Exp,
                                   bias=nmax[:, h, qb:qb + 1], accum_out=psum_p[:, h, qb:qb + 1])\
                       .then_inc(S["exp_done"], 1)

            def probs_turned(h):
                act.wait_ge(S["pT_done"], h + 1)
                act.activation(probT[:, h, :], bank[4 + h][:, 0:384], ACT.Copy).then_inc(S["pT_read"], 1)

            exps(0)
            exps(1)
            read_unit(5)
            act.activation(zv[:, :, :].rearrange("p b c -> p (b c)"), ub(5)[:, :], ACT.Copy)\
               .then_inc(unit_read[1], 1)
            exps(2)
            exps(3)
            read_unit(6)
            act.activation(zu[:, :, :].rearrange("p b c -> p (b c)"), ub(6)[:, :], ACT.Copy)\
               .then_inc(unit_read[0], 1)
            probs_turned(0)
            probs_turned(1)
            read_unit(7)
            act.activation(zp[:, :, PP:PP + T], ub(7)[:, :].rearrange("p (j t) -> p j t", j=2), ACT.Copy)\
               .then_inc(unit_read[1], 1)
            act.wait_ge(S["tv_done"], 1)
            act.activation(tv[:, :, :], tv[:, :, :], ACT.Sigmoid).then_inc(S["sigv_done"], 1)
            act.wait_ge(S["tu_done"], 1)
            act.activation(tu[:, :, :], tu[:, :, :], ACT.Sigmoid).then_inc(S["sigu_done"], 1)
            probs_turned(2)
            probs_turned(3)
            act.wait_ge(S["v_var"], 1)
            act.activation(rstd[:, 14:16], rstd[:, 12:14], ACT.Sqrt).then_inc(S["v_rstd"], 1)
            act.wait_ge(S["av_done"], 1)
            act.activation(y[:, 3, :, :].rearrange("p j t -> p (j t)"), bank[4][:, :], ACT.Copy).then_inc(S["av_y"], 1)

            def cast_out(m):
                act.wait_ge(S["cast_done"], m + 1)
                if m == 0:
                    act.wait_ge(S["sg_y"], 1)
                which, cols = m // 2, slice((m % 2) * 512, (m % 2 + 1) * 512)
                if which != 2:
                    act.activation([gate_m, shift_f, None, gate_f][which][:, cols], bank[B_CAST][:, :], ACT.Copy)\
                       .then_inc(S["cast_read"], 1)

            for g in range(N_GATE):
                read_unit(8 + g)
                if g >= LAG + 2:
                    act.wait_ge(S["gb_done"], g - LAG - 1)
                act.activation(sig[:, g % (LAG + 2), :], ub(g)[:, :], ACT.Sigmoid).then_inc(unit_read[g % 2], 1)
                if g % 2 == 0 and g:
                    cast_out(g // 2 - 1)
                if g % 2:
                    m = g // 2
                    act.wait_ge(S["ada_done"], 8 + g + 1)
                    if m >= 2:
                        act.wait_ge(S["cast_done"], m - 1)
                    act.activation(part2[:, m % 2, :], bank[B_ADA][:, :], ACT.Copy).then_inc(S["part2_done"], 1)
                if g == CONV_AT:
                    act.wait_ge(S["conv_var"], 1)
                    act.activation(mean_c[:, :], rs_c[:, :], ACT.Sqrt).then_inc(S["conv_rstd"], 1)
                    act.wait_ge(S["conv_n"], 2)
                    act.activation(sq_c[:, :, :], conv[:, :, :], ACT.Sigmoid).then_inc(S["conv_sig"], 1)
            cast_out(7)
            for tb in range(TB):
                for k in (2 * tb, 2 * tb + 1):
                    cols = slice((k % 2) * 512, (k % 2 + 1) * 512)
                    act.wait_ge(S["x2_done"], k + 1)
                    act.activation(junk[:, cols], x_sb[:, tb, cols], ACT.Square, accum_out=ssq[:, 4 + k:5 + k])\
                       .then_inc(S["x2_sq"], 1)
                act.wait_ge(S["x2_var"], tb + 1)
                act.activation(rstd[:, 6 + tb:7 + tb], rstd[:, 4 + tb:5 + tb], ACT.Sqrt).then_inc(S["x2_rstd"], 1)
            for tb in range(TB):
                for q in range(2):
                    act.wait_ge(S["h2T_done"], 2 * tb + q + 1)
                    act.activation(hT[:, 4 * q:4 * q + 4, tb * P:(tb + 1) * P],
                                   bank[OUT_BANK[2 * tb + q]][:, :].rearrange("p (k t) -> p k t", k=4), ACT.Copy)\
                       .then_inc(S["h2T_read"], 1)

            def h_part(i):
                act.activation(parts[i], h2, ACT.Copy).then_inc(S["part_done"], 1)

            h_part(0)
            act.wait_ge(S["sc_mm"], 1)
            act.activation(score[:, :, :].rearrange("p b e -> p (b e)"), bank[4][:, 0:TB * E], ACT.Sigmoid)\
               .then_inc(S["score_done"], 1)
            act.wait_ge(S["rest_done"], 1)
            h_part(1)
            for tb in range(TB):
                act.wait_ge(S["sh_done"], tb + 1)
                act.activation(hid_s[:, tb, :], bank[5 + tb][:, 0:FF], ACT.Sigmoid).then_inc(S["sh_sig"], 1)
            act.wait_ge(S["rest_done"], 2)
            h_part(2)
            for q in range(2):
                act.wait_ge(S["gathered"], q + 1)
                act.activation(xg[:, 0, 4 * q:4 * q + 4, :].rearrange("p k s -> p (k s)"), bank[B_GATH][:, :], ACT.Copy)\
                   .then_inc(S["gath_read"], 1)
            act.wait_ge(S["sh_T"], 1)
            act.activation(hidT_s[:, :, :, :].rearrange("p b j t -> p (b j t)"), bank[7][:, :], ACT.Copy)\
               .then_inc(S["sh_TT"], 1)
            act.wait_ge(S["npass_done"], 1)
            passes = act.value_load(n_pass[0:1, 0:1], min_val=1, max_val=MAX_PASS)
            with act.Fori(0, passes) as ps:
                with act.Fori(0, PAIRS // RING_PAIRS) as it:
                    for r in range(RING_PAIRS):
                        use = ps * (PAIRS // RING_PAIRS) + it
                        n = use * RING_PAIRS + r
                        nxt = (r + 1) % 2

                        def copy_gathered(q):
                            act.wait_ge(S["gathered"], 2 * n + (3 + q))
                            act.activation(xg[:, nxt, 4 * q:4 * q + 4, :].rearrange("p k s -> p (k s)"),
                                           bank[B_GATH][:, :], ACT.Copy).then_inc(S["gath_read"], 1)

                        copy_gathered(0)
                        act.wait_ge(w13_used[r], use + 2)
                        act.activation(sg1[:, :], bank[B_HID][:, 0:FF], ACT.Sigmoid).then_inc(S["sig1_done"], 1)
                        copy_gathered(1)
                        act.wait_ge(S["turn_done"], n + 1)
                        act.activation(turned[:, r, :, :].rearrange("p k s -> p (k s)"), bank[B_HID][:, :], ACT.Copy)\
                           .then_inc(S["turn_read"], 1)
            for tb in range(TB):
                for k in (2 * tb, 2 * tb + 1):
                    cols = slice((k % 2) * 512, (k % 2 + 1) * 512)
                    act.wait_ge(S["x3_done"], k + 1)
                    act.activation(junk[:, cols], x_sb[:, tb, cols], ACT.Square, accum_out=ssq[:, k:k + 1])\
                       .then_inc(S["x3_sq"], 1)
                act.wait_ge(S["x3_var"], tb + 1)
                act.activation(rstd[:, 10 + tb:11 + tb], rstd[:, 8 + tb:9 + tb], ACT.Sqrt).then_inc(S["x3_rstd"], 1)

        @block.vector
        def _(dve):
            link = linker(dve, S["v_step"])
            dve.wait_ge(S["x_sq"], 1)
            link(dve.tensor_scalar(rstd[:, 0:2], ssq[:, 2:4], EPS, None, ALU.add))
            dve.reciprocal(rstd[:, 0:2], rstd[:, 0:2]).then_inc(S["x_var"], 1)
            dve.wait_ge(S["c_sig"], 1)
            link(dve.tensor_tensor(cact[:, :], csig[:, :], pr("c"), ALU.mult))
            dve.tensor_copy(crep[:, :, :], cact[:, :].unsqueeze(2).to_broadcast([P, KD, 32])).then_inc(S["c_rep"], 1)
            dve.wait_ge(S["x_rstd"], 1)
            for tb in range(TB):
                dve.tensor_scalar(xn[:, tb, :], x_sb[:, tb, :], rstd[:, 2 + tb:3 + tb], None, ALU.mult)\
                   .then_inc(S["xn_done"], 1)
            dve.wait_ge(S["vec_done"], 1)
            dve.scalar_tensor_tensor(out=a_c[:, :], in0=bank[0][:, KD:2 * KD], scalar=1.0, in1=pr("mix_g"),
                                     op0=ALU.add, op1=ALU.mult).then_inc(S["ac_done"], 1)
            dve.tensor_copy(s_c[:, :], bank[0][:, 0:KD]).then_inc(S["ac_done"], 1)
            dve.wait_ge(S["ac_done"], 2)
            dve.wait_ge(S["xT_done"], 2 * KD)
            for k in range(4):
                dve.tensor_scalar(hT[:, k, :], bank[4 + k // 2][:, (k % 2) * 256:(k % 2 + 1) * 256], a_c[:, k:k + 1],
                                  s_c[:, k:k + 1], ALU.mult, ALU.add).then_inc(S["h_done"], 1)
            dve.wait_ge(S["misc_in"], 32)
            for h in range(HEADS):
                dve.tensor_tensor(sgw[:, h, :], sgw[:, h, :], cn("upper"), ALU.mult).then_inc(S["sgw_done"], 1)
            dve.wait_ge(S["unit_done"], 2)
            dve.wait_ge(unit_read[0], 1)
            dve.wait_ge(S["p_step"], 1)
            dve.tensor_tensor(glu[:, :, PAD:PAD + T], bank[1][:, :].rearrange("p (j t) -> p j t", j=2),
                              sig_c[:, :, :], ALU.mult).then_inc(unit_read[1], 1)
            dve.wait_ge(S["f_done"], 1)
            dve.tensor_scalar(fz[:, 0, :], bank[7][0:HEADS, 0:T], par[0:HEADS, P_AT["b_f"]:P_AT["b_f"] + 1], None,
                              ALU.add).then_inc(S["f_read"], 1)
            dve.wait_ge(S["f_read"], 1)
            dve.scalar_tensor_tensor(out=fz[:, 1, :], in0=fz[:, 0, :], scalar=-1.0, in1=fz[:, 0, :],
                                     op0=ALU.mult, op1=ALU.max).then_inc(S["f_read"], 1)
            dve.wait_ge(S["exp_f"], 1)
            link(dve.scalar_tensor_tensor(out=fz[:, 2, :], in0=fz[:, 0, :], scalar=0.0, in1=fz[:, 1, :],
                                          op0=ALU.min, op1=ALU.subtract))
            dve.tensor_tensor_scan(fz[:, 0, :], const[0:HEADS, C_AT["ones"]:C_AT["ones"] + T], fz[:, 2, :], 0.0,
                                   ALU.mult, ALU.add).then_inc(S["cum_done"], 1)
            dve.wait_ge(S["cum_done"], 1)
            dve.tensor_scalar(fz[:, 1, :], fz[:, 0, :], -1.0, None, ALU.mult).then_inc(S["cum_done"], 1)

            dve.wait_ge(unit_read[1], 1)
            for i in range(TAPS):
                for j in range(2):
                    w = pr("conv_w", j * TAPS + i, j * TAPS + i + 1)
                    src = glu[:, j, i:i + T]
                    if i:
                        dve.wait_ge(S["conv_done"], 2 * i + j - 1)
                        ins = dve.scalar_tensor_tensor(out=conv[:, j, :], in0=src, scalar=w, in1=conv[:, j, :],
                                                       op0=ALU.mult, op1=ALU.add)
                    else:
                        ins = dve.tensor_scalar(conv[:, j, :], src, w, pr("conv_b", j, j + 1), ALU.mult, ALU.add)
                    ins.then_inc(S["conv_done"], 1)

            def mask_and_max(h):
                dve.wait_ge(S["logits_done"], h + 1)
                if h >= 2:
                    dve.wait_ge(S["exp_done"], 2 * (h - 1))
                dve.tensor_tensor(logit[:, h % 2, :], bank[4 + h][:, 0:384], cn("mask"), ALU.add)\
                   .then_inc(S["logit_done"], 1)
                dve.wait_ge(S["logit_done"], 3 * h + 1)
                for qb in range(2):
                    lo, n = (0, P) if qb == 0 else (P, T)
                    dve.tensor_reduce(nmax[:, h, qb:qb + 1], logit[:, h % 2, lo:lo + n], AX, ALU.max, negate=True)\
                       .then_inc(S["logit_done"], 1)

            def normalise(h):
                dve.wait_ge(S["exp_done"], 2 * (h + 1))
                link(dve.reciprocal(rden[:, h, :], psum_p[:, h, :]))
                for qb in range(2):
                    lo, n = (0, P) if qb == 0 else (P, T)
                    dve.tensor_scalar(prob[:, h, lo:lo + n], prob[:, h, lo:lo + n], rden[:, h, qb:qb + 1], None, ALU.mult)\
                       .then_inc(S["prob_done"], 1)

            mask_and_max(0)
            mask_and_max(1)
            normalise(0)
            normalise(1)
            mask_and_max(2)
            mask_and_max(3)
            normalise(2)
            normalise(3)

            def gelu_inner(t, z):
                link(dve.tensor_tensor(t, z, z, ALU.mult))
                link(dve.tensor_scalar(t, t, 1.5957691216057308 * 0.044715, 1.5957691216057308, ALU.mult, ALU.add))
                return dve.tensor_tensor(t, t, z, ALU.mult)

            dve.wait_ge(unit_read[1], 3)
            gelu_inner(tv[:, :, :], zv[:, :, :]).then_inc(S["tv_done"], 1)
            dve.wait_ge(unit_read[0], 4)
            gelu_inner(tu[:, :, :], zu[:, :, :]).then_inc(S["tu_done"], 1)
            dve.wait_ge(S["sigv_done"], 1)
            link(dve.tensor_tensor(zv[:, :, :], zv[:, :, :], tv[:, :, :], ALU.mult))
            for tb in range(TB):
                link(dve.bn_stats(stats[:, tb, :], zv[:, tb, :]))
                link(dve.bn_aggr(mv[:, tb, :], stats[:, tb, :]))
            link(dve.tensor_scalar(rstd[:, 12:14], mv[:, :, 1], EPS, None, ALU.add))
            dve.reciprocal(rstd[:, 12:14], rstd[:, 12:14]).then_inc(S["v_var"], 1)
            dve.wait_ge(unit_read[1], 4)
            dve.wait_ge(S["zero_done"], 6)
            link(dve.tensor_tensor(w2s[:, :, 1:], zp[:, :, 1:], zp[:, :, 0:PP + T - 1], ALU.add))
            link(dve.tensor_tensor(w4s[:, :, 2:], w2s[:, :, 2:], w2s[:, :, 0:PP + T - 2], ALU.add))
            link(dve.tensor_tensor(w8s[:, 4:], w4s[:, 1, 4:], w4s[:, 1, 0:PP + T - 4], ALU.add))
            inv = cn("inv").rearrange("p (j t) -> p j t", j=2)
            link(dve.tensor_tensor(pooled[0:64, 0, :], w2s[0:64, 0, PP:], inv[0:64, 0, :], ALU.mult))
            link(dve.tensor_tensor(pooled[64:P, 0, :], w4s[64:P, 0, PP:], inv[64:P, 0, :], ALU.mult))
            link(dve.tensor_tensor(pooled[0:64, 1, :], w8s[0:64, PP:], inv[0:64, 1, :], ALU.mult))
            link(dve.tensor_tensor(pooled[64:P, 1, :], w8s[64:P, PP:], w8s[64:P, PP - 8:PP + T - 8], ALU.add))
            link(dve.tensor_tensor(pooled[64:P, 1, :], pooled[64:P, 1, :], inv[64:P, 1, :], ALU.mult))
            dve.tensor_tensor(pooled[:, :, :], pooled[:, :, :], zp[:, :, PP:], ALU.subtract).then_inc(S["pooled_done"], 1)
            dve.wait_ge(S["v_rstd"], 1)
            for tb in range(TB):
                link(dve.tensor_scalar(zv[:, tb, :], zv[:, tb, :], mv[:, tb, 0:1], rstd[:, 14 + tb:15 + tb],
                                       ALU.subtract, ALU.mult))
                link(dve.tensor_tensor(zv[:, tb, :], zv[:, tb, :], sg_g[:, :], ALU.mult))
                dve.tensor_tensor(zv[:, tb, :], zv[:, tb, :], sg_beta[:, :], ALU.add).then_inc(S["vn_done"], 1)
            dve.wait_ge(S["sigu_done"], 1)
            link(dve.tensor_tensor(zu[:, :, :], zu[:, :, :], tu[:, :, :], ALU.mult))
            dve.wait_ge(S["sg_done"], 1)
            link(dve.tensor_tensor(tu[:, :, :], bank[5][:, :].rearrange("p (j t) -> p j t", j=2), sg_bias[:, :, :], ALU.add))
            dve.tensor_tensor(y[:, 1, :, :], tu[:, :, :], zu[:, :, :], ALU.mult).then_inc(S["sg_y"], 1)
            dve.wait_ge(S["pool_mm"], 1)
            for j in range(2):
                dve.tensor_scalar(y[:, 0, j, :], bank[6][:, j * T:(j + 1) * T], pr("pool_scale", j, j + 1), None, ALU.mult)\
                   .then_inc(S["pool_y"], 1)

            def conv_norm_1():
                dve.wait_ge(S["csum_done"], 1)
                link(dve.tensor_scalar(mean_c[:, :], bank[7][:, 0:T], 1.0 / BW, None, ALU.mult))
                for j in range(2):
                    link(dve.tensor_tensor(conv[:, j, :], conv[:, j, :], mean_c[:, :], ALU.subtract))
                dve.tensor_tensor(sq_c[:, :, :], conv[:, :, :], conv[:, :, :], ALU.mult).then_inc(S["conv_c"], 1)

            def conv_norm_2():
                dve.wait_ge(S["cvar_done"], 1)
                link(dve.tensor_scalar(rs_c[:, :], bank[6][:, 0:T], 1.0 / BW, EPS, ALU.mult, ALU.add))
                dve.reciprocal(rs_c[:, :], rs_c[:, :]).then_inc(S["conv_var"], 1)

            def merge(g):
                dc, n = g // 4, g % 4
                dve.wait_ge(S["branch_done"], g + 1)
                dst = merged[:, 2 * dc:2 * dc + 2, :].rearrange("p k t -> p (k t)")
                o = dst if n == 0 else gb[:, :]
                if n and 3 * dc + n > 1:
                    dve.wait_ge(S["merged_done"], 3 * dc + n - 1)
                dve.tensor_tensor(o, bank[4 + g % 2][:, :], sig[:, g % (LAG + 2), :], ALU.mult).then_inc(S["gb_done"], 1)
                if n:
                    dve.wait_ge(S["gb_done"], g + 1)
                    dve.tensor_tensor(dst, dst, gb[:, :], ALU.add).then_inc(S["merged_done"], 1)

            def scale_rows(hf):
                cols = slice(hf * 512, (hf + 1) * 512)
                dve.wait_ge(S["cast_done"], 5 + hf)
                dve.wait_ge(S["late_in"], 48)
                dve.scalar_tensor_tensor(out=scale_f[:, cols], in0=bank[B_CAST][:, :], scalar=1.0, in1=scale_f[:, cols],
                                         op0=ALU.add, op1=ALU.mult).then_inc(S["cast_read"], 1)

            conv_norm_1()
            conv_norm_2()
            dve.wait_ge(S["conv_rstd"], 1)
            for j in range(2):
                link(dve.tensor_tensor(conv[:, j, :], conv[:, j, :], mean_c[:, :], ALU.mult))
                dve.tensor_scalar(conv[:, j, :], conv[:, j, :], pr("conv_g", j, j + 1), pr("conv_beta", j, j + 1),
                                  ALU.mult, ALU.add).then_inc(S["conv_n"], 1)
            dve.wait_ge(S["conv_sig"], 1)
            dve.tensor_tensor(y[:, 2, :, :], conv[:, :, :], sq_c[:, :, :], ALU.mult).then_inc(S["conv_y"], 1)
            for g in range(N_GATE):
                merge(g)
                if g == 10 - LAG:
                    scale_rows(0)
                if g == 12 - LAG:
                    scale_rows(1)
            for tb in range(TB):
                for k in (2 * tb, 2 * tb + 1):
                    cols = slice((k % 2) * 512, (k % 2 + 1) * 512)
                    dve.wait_ge(S["out_mm"], k + 1)
                    if k == 0:
                        dve.wait_ge(S["cast_read"], 2)
                    if k:
                        dve.wait_ge(S["x2_done"], k)
                    link(dve.tensor_tensor(gb[:, :], bank[OUT_BANK[k]][:, :], gate_m[:, cols], ALU.mult))
                    dve.tensor_tensor(x_sb[:, tb, cols], x_sb[:, tb, cols], gb[:, :], ALU.add).then_inc(S["x2_done"], 1)
                dve.wait_ge(S["x2_sq"], 2 * tb + 2)
                link(dve.tensor_tensor(rstd[:, 4 + tb:5 + tb], ssq[:, 4 + 2 * tb:5 + 2 * tb],
                                       ssq[:, 5 + 2 * tb:6 + 2 * tb], ALU.add))
                link(dve.tensor_scalar(rstd[:, 4 + tb:5 + tb], rstd[:, 4 + tb:5 + tb], 1.0 / D, EPS, ALU.mult, ALU.add))
                dve.reciprocal(rstd[:, 4 + tb:5 + tb], rstd[:, 4 + tb:5 + tb]).then_inc(S["x2_var"], 1)
                dve.wait_ge(S["x2_rstd"], tb + 1)
                link(dve.scalar_tensor_tensor(out=h2[:, tb, :], in0=x_sb[:, tb, :], scalar=rstd[:, 6 + tb:7 + tb],
                                              in1=scale_f[:, :], op0=ALU.mult, op1=ALU.mult))
                dve.tensor_tensor(h2[:, tb, :], h2[:, tb, :], shift_f[:, :], ALU.add).then_inc(S["h2_done"], 1)

            def pick(vals, n, k, m_gt, m_eq, m_pre):
                for tb in range(TB):
                    link(dve.max(top8[:, tb, :], vals[:, tb, :]))
                kth = top8[:, :, k - 1:k].to_broadcast([P, TB, n])
                link(dve.tensor_tensor(m_gt, vals, kth, ALU.is_gt))
                link(dve.tensor_tensor(m_eq, vals, kth, ALU.is_equal))
                link(dve.tensor_reduce(need[:, :], m_gt, AX, ALU.add))
                link(dve.tensor_scalar(need[:, :], need[:, :], -1.0, float(k), ALU.mult, ALU.add))
                for tb in range(TB):
                    link(dve.tensor_tensor_scan(m_pre[:, tb, :], cn("ones", 0, n), m_eq[:, tb, :], 0.0, ALU.mult, ALU.add))
                link(dve.tensor_tensor(m_pre, m_pre, need[:, :].unsqueeze(2).to_broadcast([P, TB, n]), ALU.is_le))
                link(dve.tensor_tensor(m_eq, m_eq, m_pre, ALU.mult))
                return dve.tensor_tensor(m_gt, m_gt, m_eq, ALU.add)

            dve.wait_ge(S["score_done"], 1)
            link(dve.tensor_tensor(sel[:, :, :], score[:, :, :], r_bias[:, :].unsqueeze(1).to_broadcast([P, TB, E]), ALU.add))
            for tb in range(TB):
                for g in range(GROUPS):
                    ins = dve.max(top[:, tb, g, :], sel[:, tb, 8 * g:8 * g + 8])
            link(ins)
            link(dve.tensor_tensor(gs[:, :, :], top[:, :, :, 0], top[:, :, :, 1], ALU.add))
            link(pick(gs[:, :, :], GROUPS, TOPG, gt_g[:, :, :], eq_g[:, :, :], pre_g[:, :, :]))
            link(dve.tensor_scalar(gt_g[:, :, :], gt_g[:, :, :], -NEG, NEG, ALU.mult, ALU.add))
            link(dve.tensor_tensor(sel[:, :, :].rearrange("p b (g i) -> p (b g) i", g=GROUPS),
                                   sel[:, :, :].rearrange("p b (g i) -> p (b g) i", g=GROUPS),
                                   gt_g[:, :, :].rearrange("p b g -> p (b g)").unsqueeze(2).to_broadcast([P, TB * GROUPS, 8]),
                                   ALU.add))
            pick(sel[:, :, :], E, TOPK, picked[:, :, :], eq[:, :, :], pre[:, :, :]).then_inc(S["picked_done"], 1)
            dve.wait_ge(S["picked_done"], 1)
            link(dve.tensor_tensor(gt[:, :, :], score[:, :, :], picked[:, :, :], ALU.mult))
            link(dve.tensor_reduce(wsum[:, :], gt[:, :, :], AX, ALU.add))
            link(dve.reciprocal(wsum[:, :], wsum[:, :]))
            link(dve.tensor_scalar(wsum[:, :], wsum[:, :], ROUTE_SCALE, None, ALU.mult))
            link(dve.tensor_tensor(gates[:, :, 0:E], gt[:, :, :], wsum[:, :].unsqueeze(2).to_broadcast([P, TB, E]), ALU.mult))
            link(dve.tensor_copy(gates[:, :, E:EP], gates[:, :, 0:4]))
            dve.wait_ge(S["rank_done"], 1)
            link(dve.scalar_tensor_tensor(out=pos[:, :, 0:E], in0=bank[4][:, 0:TB * E].rearrange("p (b e) -> p b e", b=TB),
                                          scalar=1.0, in1=picked[:, :, :], op0=ALU.add, op1=ALU.mult))
            link(dve.tensor_scalar(pos[:, :, 0:E], pos[:, :, 0:E], -1.0, None, ALU.add))
            link(dve.tensor_scalar(pos[:, :, E:EP], pos[:, :, 0:4], -float(CAP), None, ALU.add))
            link(dve.tensor_reduce(most[:, :], bank[4][:, TB * E:(TB + 1) * E], AX, ALU.max))
            link(dve.tensor_tensor(over[:, :], most[:, 0:1].to_broadcast([P, 3]), cn("thr"), ALU.is_gt))
            link(dve.tensor_reduce(most[:, :], over[:, :], AX, ALU.add))
            dve.tensor_scalar(n_pass[:, :], most[:, :], 1.0, None, ALU.add).then_inc(S["npass_done"], 1)

            iota = cn("iota").unsqueeze(1).to_broadcast([P, 2, CAP])

            def build(b, first, dyn, count):
                for tb in range(TB):
                    sl = bass.ds(first, 2) if dyn else slice(first, first + 2)
                    pp = pos[:, tb, sl].unsqueeze(2).to_broadcast([P, 2, CAP])
                    dve.tensor_tensor(take[:, b, tb, :].rearrange("p (e s) -> p e s", e=2), iota, pp, ALU.is_equal)\
                       .then_inc(S["take_raw"], 1)
                for tb in range(TB):
                    sl = bass.ds(first, 2) if dyn else slice(first, first + 2)
                    gg = gates[:, tb, sl].unsqueeze(2).to_broadcast([P, 2, CAP])
                    dve.wait_ge(S["take_raw"], count * 2 + (tb + 1))
                    dve.tensor_tensor(gtake[:, b, tb, :].rearrange("p (e s) -> p e s", e=2),
                                      take[:, b, tb, :].rearrange("p (e s) -> p e s", e=2), gg, ALU.mult)\
                       .then_inc(S["take_built"], 1)

            build(0, 0, False, 0)
            build(1, 2, False, 1)
            for tb in range(TB):
                dve.wait_ge(S["sh_sig"], tb + 1)
                link(dve.tensor_tensor(hid_s[:, tb, :], hid_s[:, tb, :], bank[5 + tb][:, 0:FF], ALU.mult))
                dve.tensor_tensor(hid_s[:, tb, :], hid_s[:, tb, :], bank[5 + tb][:, FF:2 * FF], ALU.mult)\
                   .then_inc(S["sh_hid"], 1)
            link(dve.memset(turned[:, 1, 2:4, :], 0.0))
            dve.memset(y_sb[:, :], 0.0).then_inc(S["y_read"], 2)
            passes = dve.value_load(n_pass[0:1, 0:1], min_val=1, max_val=MAX_PASS)
            with dve.Fori(0, passes) as ps:
                with dve.Fori(0, PAIRS // RING_PAIRS) as it:
                    for r in range(RING_PAIRS):
                        use = ps * (PAIRS // RING_PAIRS) + it
                        n = use * RING_PAIRS + r
                        dve.wait_ge(S["sig1_done"], n + 1)
                        dve.tensor_tensor(th[:, :], sg1[:, :], bank[B_HID][:, 0:FF], ALU.mult).then_inc(S["th_done"], 1)
                        dve.wait_ge(S["th_done"], n + 1)
                        dve.tensor_tensor(hid[:, :], th[:, :], bank[B_HID][:, FF:2 * FF], ALU.mult)\
                           .then_inc(S["hid_done"], 1)
                        dve.wait_ge(S["turn_done"], n + 1)
                        build(r, it * (2 * RING_PAIRS) + (2 * r + 4), True, n + 2)
                        dve.wait_ge(S["y0_done"], n + 1)
                        dve.tensor_copy(y_sb[:, 0:512], bank[B_Y[0]][:, :]).then_inc(S["y_read"], 1)
                        dve.wait_ge(w2_used[r], use + 2)
                        dve.tensor_copy(y_sb[:, 512:D], bank[B_Y[1]][:, :]).then_inc(S["y_read"], 1)
                dve.wait_ge(S["take_built"], (ps + 1) * (2 * PAIRS) + 4)
                dve.tensor_scalar(pos[:, :, :], pos[:, :, :], -float(CAP), None, ALU.add).then_inc(S["pos_next"], 1)
                dve.wait_ge(S["pos_next"], ps + 1)
            dve.wait_ge(S["final_in"], 16)
            for tb in range(TB):
                for k in (2 * tb, 2 * tb + 1):
                    cols = slice((k % 2) * 512, (k % 2 + 1) * 512)
                    dve.wait_ge(S["sum_done"], k + 1)
                    if k == 0:
                        dve.wait_ge(S["cast_read"], 8)
                    if k:
                        dve.wait_ge(S["x3_done"], k)
                    link(dve.tensor_tensor(gb[:, :], bank[B_OUT[k]][:, :], gate_f[:, cols], ALU.mult))
                    dve.tensor_tensor(x_sb[:, tb, cols], x_sb[:, tb, cols], gb[:, :], ALU.add).then_inc(S["x3_done"], 1)
                dve.wait_ge(S["x3_sq"], 2 * tb + 2)
                link(dve.tensor_tensor(rstd[:, 8 + tb:9 + tb], ssq[:, 2 * tb:1 + 2 * tb], ssq[:, 1 + 2 * tb:2 + 2 * tb], ALU.add))
                link(dve.tensor_scalar(rstd[:, 8 + tb:9 + tb], rstd[:, 8 + tb:9 + tb], 1.0 / D, EPS, ALU.mult, ALU.add))
                dve.reciprocal(rstd[:, 8 + tb:9 + tb], rstd[:, 8 + tb:9 + tb]).then_inc(S["x3_var"], 1)
                dve.wait_ge(S["x3_rstd"], tb + 1)
                for hf in range(2):
                    cols = slice(hf * 512, (hf + 1) * 512)
                    dve.scalar_tensor_tensor(out=h2[:, tb, cols], in0=x_sb[:, tb, cols], scalar=rstd[:, 10 + tb:11 + tb],
                                             in1=final_g[:, cols], op0=ALU.mult, op1=ALU.mult).then_inc(S["fin_done"], 1)

        @block.tensor
        def _(pe):
            def mm(o, lhsT, rhs, start=True, stop=True):
                return pe.matmul(o, lhsT, rhs, start=start, stop=stop, skip_group_check=True)

            def ready(u):
                pe.wait_ge(landed[SLOT[u]], 16 * (FILLS[u] + 1))

            pe.wait_ge(S["const_in"], 16)

            def ada(i, b):
                u = ("ada", i)
                ready(u)
                w = unit(u).rearrange("p (k n) -> p k n", k=KD)
                cols = slice((i % 2) * 256, (i % 2 + 1) * 256)
                for k in range(KD):
                    q = 32 * (k % 4)
                    mm(bank[b][q:q + 32, cols], crep[:, k, :], w[:, k, :], start=k < 4, stop=k >= 5)
                sel_row = cn("bias_sel", i * 32, (i + 1) * 32)
                mm(bank[b][0:32, cols], sel_row, ada_b[:, :], start=False, stop=True).then_inc(S["ada_done"], 1)
            pe.wait_ge(S["c_rep"], 1)
            pe.wait_ge(S["ada_b_in"], 16)
            for i in range(3):
                ada(i, i // 2)
            for tb in range(TB):
                pe.wait_ge(S["xn_done"], tb + 1)
                for k in range(KD):
                    pe.transpose(bank[4 + k // 2][:, (k % 2) * T + tb * P:(k % 2) * T + (tb + 1) * P],
                                 xn[:, tb, k::KD],
                                 ident).then_inc(S["xT_done"], 1)
            for i in range(3, 8):
                ada(i, i // 2)
            pe.wait_ge(S["ada_read"], 4)
            for v in range(2):
                for k in range(KD):
                    ins = mm(bank[0][:, v * KD + k:v * KD + k + 1], part[:, v, k::KD], cn("rows4", 0, 1))
            ins.then_inc(S["vec_done"], 1)

            def begin_unit(i, u):
                ready(u)
                if i >= 2:
                    pe.wait_ge(unit_read[i % 2], i // 2)
                return bank[B_UNIT[i % 2]], unit(u).rearrange("p (k n) -> p k n", k=KD)

            def channels(i, u):
                b, w = begin_unit(i, u)
                for m in range(2):
                    for k in range(KD):
                        ins = mm(b[:, m * T:(m + 1) * T], w[:, k, m * P:(m + 1) * P], hT[:, k, :], k == 0, k == KD - 1)
                ins.then_inc(S["unit_done"], 1)

            def tokens(i, u):
                b, w = begin_unit(i, u)
                for tb in range(TB):
                    for k in range(KD):
                        ins = mm(b[:, tb * BW:(tb + 1) * BW], hT[:, k, tb * P:(tb + 1) * P], w[:, k, :], k == 0, k == KD - 1)
                ins.then_inc(S["unit_done"], 1)

            def logits(h):
                b = bank[4 + h]
                mm(b[:, 0:P], qa[:, h, 0:P], ka[:, h, 0:P])
                mm(b[:, P:P + T], qa[:, h, P:T], ka[:, h, :]).then_inc(S["logits_done"], 1)

            def turn_probs(h):
                pe.wait_ge(S["prob_done"], 2 * h + 2)
                for q in range(3):
                    ins = pe.transpose(bank[4 + h][:, q * P:(q + 1) * P], prob[:, h, q * P:(q + 1) * P], ident)
                ins.then_inc(S["pT_done"], 1)

            pe.wait_ge(S["h_done"], 8)
            channels(0, ("mix", 0))
            channels(1, ("mix", 1))
            pe.wait_ge(S["misc_in"], 32)
            for k in range(KD):
                ins = mm(bank[7][0:HEADS, 0:T], wf[:, k, :], hT[:, k, :], k == 0, k == KD - 1)
            ins.then_inc(S["f_done"], 1)
            channels(2, ("mix", 2))
            channels(3, ("mix", 3))
            tokens(4, ("mix", 4))
            pe.wait_ge(unit_read[0], 2)
            pe.wait_ge(unit_read[1], 2)
            pe.wait_ge(S["cum_rows"], 32)
            for h in range(HEADS):
                logits(h)
            tokens(5, ("mix", 5))
            channels(6, ("mix", 6))
            turn_probs(0)
            turn_probs(1)
            channels(7, ("mix", 7))
            turn_probs(2)
            turn_probs(3)

            def attend():
                pe.wait_ge(unit_read[0], 3)
                for h in range(HEADS):
                    pe.wait_ge(S["pT_read"], HEADS if h == 0 else h + 1)
                    lo, c = 64 * (h % 2), (h // 2) * T
                    vh = slice(h * HD, (h + 1) * HD)
                    mm(bank[4][lo:lo + HD, c:c + P], v_sb[:, 0, vh], probT[:, h, 0:P])
                    mm(bank[4][lo:lo + HD, c + P:c + T], v_sb[:, 0, vh], probT[:, h, P:T], True, False)
                    ins = mm(bank[4][lo:lo + HD, c + P:c + T], v_sb[:, 1, vh], probT[:, h, T:T + P], False, True)
                ins.then_inc(S["av_done"], 1)

            def spatial():
                pe.wait_ge(S["vn_done"], TB)
                pe.wait_ge(S["sgw_done"], HEADS)
                for h in range(HEADS):
                    lo, c = 64 * (h % 2), (h // 2) * T
                    for tb in range(TB):
                        ins = mm(bank[5][lo:lo + HD, c + tb * P:c + (tb + 1) * P], zv[:, tb, h * HD:(h + 1) * HD],
                                 sgw[:, h, :])
                ins.then_inc(S["sg_done"], 1)

            def pool_linear():
                pe.wait_ge(S["pooled_done"], 1)
                for j in range(2):
                    ins = mm(bank[6][:, j * T:(j + 1) * T], pool_w[:, j, :], pooled[:, j, :])
                ins.then_inc(S["pool_mm"], 1)

            def channel_sum(b, src, done):
                for j in range(2):
                    ins = mm(b[:, 0:T], cn("ones", 0, P), src[:, j, :], j == 0, j == 1)
                ins.then_inc(done, 1)

            def cast(m):
                pe.wait_ge(S["part2_done"], m + 1)
                if m:
                    pe.wait_ge(S["cast_read"], m)
                mm(bank[B_CAST][:, :], cn("rows4"), part2[:, m % 2, :]).then_inc(S["cast_done"], 1)

            def branch(g):
                dc, n = g // 4, g % 4
                b = bank[4 + g % 2]
                if n == 0:
                    ready(("branch", dc))
                if g < 4:
                    pe.wait_ge(*[(S["pool_y"], 2), (S["sg_y"], 1), (S["conv_y"], 1), (S["av_y"], 1)][n])
                if g == 0:
                    pe.wait_ge(S["av_y"], 1)
                if g >= 2:
                    pe.wait_ge(S["gb_done"], g - 1)
                w = unit(("branch", dc)).rearrange("p (n j d) -> p n j d", n=NB, j=2)
                for m in range(2):
                    for j in range(2):
                        ins = mm(b[:, m * T:(m + 1) * T], w[:, n, j, m * P:(m + 1) * P], y[:, n, j, :], j == 0, j == 1)
                ins.then_inc(S["branch_done"], 1)

            for g in range(N_GATE):
                channels(8 + g, ("gate", g))
                if g == 0:
                    attend()
                if g == 1:
                    spatial()
                    pool_linear()
                if g == CONV_AT - 1:
                    pe.wait_ge(S["conv_done"], 2 * TAPS)
                    channel_sum(bank[7], conv, S["csum_done"])
                if g == CONV_AT:
                    pe.wait_ge(S["conv_c"], 1)
                    pe.wait_ge(S["pool_y"], 2)
                    channel_sum(bank[6], sq_c, S["cvar_done"])
                if g % 2 == 0 and g:
                    cast(g // 2 - 1)
                if g % 2 == 0 and g:
                    pe.wait_ge(S["part2_done"], g // 2)
                ada(8 + g, B_ADA)
                if g >= LAG:
                    branch(g - LAG)
            cast(7)
            for g in range(N_GATE - LAG, N_GATE):
                branch(g)

            for i in range(4):
                ready(("out", i))
            for k in range(4):
                tb, hf = k // 2, k % 2
                if k == 0:
                    pe.wait_ge(S["conv_var"], 1)
                    pe.wait_ge(S["conv_c"], 1)
                if k == 2:
                    pe.wait_ge(S["gb_done"], N_GATE)
                for j in range(KD):
                    pe.wait_ge(S["merged_done"], 3 * (j // 2 + 1))
                    w = unit(("out", j // 2))
                    ins = mm(bank[OUT_BANK[k]][:, :], merged[:, j, tb * P:(tb + 1) * P],
                             w[:, (j % 2) * D + hf * 512:(j % 2) * D + (hf + 1) * 512], j == 0, j == KD - 1)
                    if k == 0 and j == 0:
                        ins.then_inc(w13_used[0], 1)
                ins.then_inc(S["out_mm"], 1)

            for tb in range(TB):
                pe.wait_ge(S["h2_done"], tb + 1)
                for q in range(2):
                    for k in range(4):
                        ins = pe.transpose(bank[OUT_BANK[2 * tb + q]][:, k * P:(k + 1) * P],
                                           h2[:, tb, 4 * q + k::KD], ident)
                    ins.then_inc(S["h2T_done"], 1)

            pe.wait_ge(S["h2T_read"], 4)
            pe.wait_ge(S["late_in"], 48)
            for tb in range(TB):
                for k in range(KD):
                    ins = mm(bank[4][:, tb * E:(tb + 1) * E], hT[:, k, tb * P:(tb + 1) * P], router[:, k, :],
                             k == 0, k == KD - 1)
                    if tb == 0 and k == 0:
                        ins.then_inc(w2_used[0], 1)
            ins.then_inc(S["sc_mm"], 1)
            for u in (("sw1", 0), ("sw3", 0)):
                ready(u)
            lo = SLOT[("sw1", 0)]
            sw13 = ring[:, lo:lo + 2, :].rearrange("p w (k f) -> p w k f", k=KD)
            for tb in range(TB):
                for k in range(KD):
                    ins = mm(bank[5 + tb][:, :].rearrange("p (w f) -> p w f", w=2), hT[:, k, tb * P:(tb + 1) * P],
                             sw13[:, :, k, :], k == 0, k == KD - 1)
                ins.then_inc(S["sh_done"], 1)
            pe.wait_ge(S["picked_done"], 1)
            mm(bank[4][:, 0:E], cn("strict"), picked[:, 0, :]).then_inc(w13_used[1], 1)
            mm(bank[4][:, E:2 * E], cn("ones", 0, P), picked[:, 0, :], True, False)
            mm(bank[4][:, E:2 * E], cn("strict"), picked[:, 1, :], False, True)
            mm(bank[4][:, 2 * E:3 * E], cn("ones", 0, P), picked[:, 0, :], True, False)
            mm(bank[4][:, 2 * E:3 * E], cn("ones", 0, P), picked[:, 1, :], False, True).then_inc(S["rank_done"], 1)

            def gather(b, q):
                for k in range(4):
                    for tb in range(TB):
                        for i in range(3):
                            ins = mm(bank[B_GATH][:, k * P:(k + 1) * P], parts[i][:, tb, 4 * q + k::KD],
                                     take[:, b, tb, :], tb == 0 and i == 0, tb == 1 and i == 2)
                ins.then_inc(S["gathered"], 1)

            pe.wait_ge(S["npass_done"], 1)
            pe.wait_ge(S["take_built"], 2)
            pe.wait_ge(S["part_done"], 3)
            gather(0, 0)
            pe.wait_ge(S["gath_read"], 1)
            gather(0, 1)
            pe.wait_ge(S["sh_hid"], TB)
            for tb in range(TB):
                for j in range(2):
                    ins = pe.transpose(bank[7][:, (2 * tb + j) * P:(2 * tb + j + 1) * P], hid_s[:, tb, j::2], ident)
            ins.then_inc(S["sh_T"], 1)
            ready(("sw2", 0))
            pe.wait_ge(S["sh_TT"], 1)
            for k in range(4):
                tb, hf = k // 2, k % 2
                for j in range(2):
                    ins = mm(bank[B_OUT[k]][:, :], hidT_s[:, tb, j, :],
                             unit(("sw2", 0))[:, j * D + hf * 512:j * D + (hf + 1) * 512], j == 0, False)
            ins.then_inc(w2_used[1], 1)

            def scatter(b, k, stop=False):
                tb, hf = k // 2, k % 2
                return mm(bank[B_OUT[k]][:, :], turned[:, b, 2 + tb, :], y_sb[:, hf * 512:(hf + 1) * 512], False, stop)

            passes = pe.value_load(n_pass[0:1, 0:1], min_val=1, max_val=MAX_PASS)
            with pe.Fori(0, passes) as ps:
                with pe.Fori(0, PAIRS // RING_PAIRS) as it:
                    for r in range(RING_PAIRS):
                        use = ps * (PAIRS // RING_PAIRS) + it
                        n = use * RING_PAIRS + r
                        nxt = (r + 1) % 2
                        pe.wait_ge(S["take_built"], 2 * n + 4)
                        pe.wait_ge(S["gath_read"], 2 * n + 2)
                        gather(nxt, 0)
                        pe.wait_ge(w13_landed[r], (use + 1) * 64)
                        w13 = ring[:, 6 * r:6 * r + 4, :].rearrange("p (e w) (k f) -> p e w k f", e=2, k=KD)
                        for k in range(KD):
                            for e in range(2):
                                q = CAP * e
                                ins = mm(bank[B_HID][q:q + CAP, :].rearrange("p (w f) -> p w f", w=2),
                                         xg[:, r, k, q:q + CAP], w13[:, e, :, k, :], k == 0, k == KD - 1)
                        ins.then_inc(w13_used[r], 1)
                        pe.wait_ge(S["gath_read"], 2 * n + 3)
                        gather(nxt, 1)
                        pe.wait_ge(S["y_read"], 2 * n + 2)
                        scatter(nxt, 0)
                        scatter(nxt, 1)
                        pe.wait_ge(S["hid_done"], n + 1)
                        for j in range(2):
                            pe.transpose(bank[B_HID][:, j * P:(j + 1) * P], hid[:, j::2], ident)
                        for tb in range(TB):
                            ins = pe.transpose(bank[B_HID][:, (2 + tb) * P:(3 + tb) * P], gtake[:, r, tb, :], ident)
                        ins.then_inc(S["turn_done"], 1)
                        scatter(nxt, 2)
                        scatter(nxt, 3)
                        pe.wait_ge(S["turn_read"], n + 1)
                        pe.wait_ge(w2_landed[r], (use + 1) * 32)
                        for hf in range(2):
                            for j in range(2):
                                for e in range(2):
                                    q = CAP * e
                                    ins = mm(bank[B_Y[hf]][q:q + CAP, :], turned[:, r, j, q:q + CAP],
                                             ring[:, 6 * r + 4 + e, j * D + hf * 512:j * D + (hf + 1) * 512], j == 0, j == 1)
                            ins.then_inc(w2_used[r] if hf else S["y0_done"], 1)
            last = passes * (2 * PAIRS)
            pe.wait_ge(S["y_read"], last + 2)
            for k in range(4):
                scatter(1, k, True).then_inc(S["sum_done"], 1)


def constants():
    import numpy as np
    c = {n: np.zeros((P, w), np.float32) for n, w in CONST.items()}
    i, j = np.arange(P)[:, None], np.arange(P)[None, :]
    c["ident"][:] = i == j
    c["upper"][:] = i <= j
    c["strict"][:] = i < j
    c["ones"][:] = 1
    c["rows4"][0::32] = 1
    causal = np.where(j <= i, 0, NEG).astype(np.float32)
    c["mask"][:, 0:P] = causal
    c["mask"][:, 2 * P:3 * P] = causal
    t = np.arange(T) + 1
    for g in range(4):
        c["inv"][64 * (g % 2):64 * (g % 2) + 64, (g // 2) * T:(g // 2 + 1) * T] = 1.0 / np.minimum(t, 2 ** (g + 1))
    c["iota"][:] = np.arange(CAP)
    c["thr"][:] = [CAP, 2 * CAP, 3 * CAP]
    for u in range(24):
        c["bias_sel"][u, 32 * u:32 * u + 32] = 1
    return np.concatenate([c[n] for n in CONST], 1)


def lay_out(inp):
    import numpy as np
    cols = [inp["c"][0].reshape(P, KD), inp["mix_norm_g"][0].reshape(P, KD)]
    cols += [inp[n][0].reshape(2, P).T for n in ("pool_scale", "conv_b", "conv_ln_g", "conv_ln_b")]
    cols.append(inp["conv_w"][0].reshape(TAPS, 2, P).transpose(2, 1, 0).reshape(P, 2 * TAPS))
    b_f = np.zeros((P, 1), np.float32)
    b_f[0:HEADS, 0] = inp["b_f"][0]
    par = np.concatenate(cols + [b_f], 1)
    wf = inp["w_in"][0][:, COL["f"]:COL["f"] + HEADS].reshape(P, KD * HEADS)
    sg_w = inp["sg_w"][0].transpose(2, 0, 1).reshape(P, HEADS * P)
    pool_w = np.zeros((P, 2, P), np.float32)
    sg_bias = np.zeros((P, 2, TB, P), np.float32)
    for g in range(4):
        lo = 64 * (g % 2)
        pool_w[lo:lo + 64, g // 2, lo:lo + 64] = inp["pool_w"][0, g]
        sg_bias[lo:lo + 64, g // 2] = inp["sg_b"][0, g]
    rows = [np.repeat(inp[n], P, 0) for n in ("sg_ln_g", "sg_ln_b")]
    misc = np.concatenate([wf, sg_w, pool_w.reshape(P, -1)] + rows + [sg_bias.reshape(P, -1)], 1)
    ada_bp = np.zeros((P, 256), np.float32)
    ada_bp[0:24] = inp["ada_b"][0].reshape(24, 256)
    return par, misc, ada_bp


_INS = ["x", "w_in", "w_branch", "w_out", "ffn_norm_g", "ada_w", "router_w", "router_bias", "exp_w1", "exp_w3", "exp_w2",
        "shared_w1", "shared_w3", "shared_w2", "final_norm_g"]


def kernel(**inputs):
    import numpy as np
    import concourse.bacc as bacc
    from concourse.bass_utils import run_bass_kernel_spmd

    nc = bacc.Bacc("TRN2", target_bir_lowering=False, num_devices=1)
    arrays = {n: np.ascontiguousarray(inputs[n]) for n in _INS}
    small = {n: np.asarray(inputs[n]) for n in ("c", "mix_norm_g", "pool_scale", "conv_b", "conv_ln_g", "conv_ln_b", "conv_w",
                                                "b_f", "w_in", "sg_w", "pool_w", "sg_b", "sg_ln_g", "sg_ln_b", "ada_b")}
    arrays["par"], arrays["misc"], arrays["ada_bp"] = lay_out(small)
    arrays["const"] = constants()
    arrays = {n + "_dram": v for n, v in arrays.items()}
    aps = {n[:-5]: nc.dram_tensor(n, v.shape, mybir.dt.from_np(v.dtype), kind="ExternalInput").ap()
           for n, v in arrays.items()}
    out = nc.dram_tensor("out_dram", (1, T, D), F32, kind="ExternalOutput").ap()
    decoder_layer(nc, aps, out)
    r = run_bass_kernel_spmd(nc, [arrays], core_ids=[0])
    return r.results[0]["out_dram"]
```

```python
from contextlib import ExitStack

import concourse.bass as bass
from concourse import mybir

F32 = mybir.dt.float32
I32 = mybir.dt.int32
BF16 = mybir.dt.bfloat16
ALU = mybir.AluOpType
ACT = mybir.ActivationFunctionType
AX = mybir.AxisListType.X

P = 128
D = 1024
T = 256
TB = T // P
KD = D // P
BW = 256
NB = 4
HEADS = 4
HD = BW // HEADS
TAPS = 31
E = 64
TOPK = 6
GROUPS = 8
TOPG = 4
ROUTE_SCALE = 2.5
FF = 256
CAP = 64
PAIRS = E // 2
MAX_PASS = T // CAP
EPS = 1e-6
NEG = -1e30

COL = {"pool": 0, "sg_u": 256, "sg_v": 512, "conv_a": 768, "conv_g": 1024, "q": 1280, "k": 1536,
       "v": 1792, "f": 2048, "gate": 2052}

RING_PAIRS = 2
SLOTS = 6 * RING_PAIRS
STEPS = PAIRS // RING_PAIRS
SPLIT = STEPS // 2
UNIT = 2048
MIX = ["conv_g", "conv_a", "q", "k", "v", "sg_v", "sg_u", "pool"]
CONV_AT = 4
LAG = 3
N_GATE = 16


def unit_plan():
    units = [("ada", i) for i in range(8)] + [("mix", i) for i in range(8)]
    for g in range(N_GATE):
        if g % 4 == 3:
            units.append(("branch", g // 4))
        units += [("gate", g), ("ada", 8 + g)]
    units += [("out", i) for i in range(4)] + [("sw1", 0), ("sw3", 0)]
    return units


UNITS = unit_plan()
SHIFT = -len(UNITS) % SLOTS
SLOT = {u: (i + SHIFT) % SLOTS for i, u in enumerate(UNITS)}
LAST = {SLOT[u]: u for u in UNITS}
BEFORE = {u: UNITS[i - SLOTS] for i, u in enumerate(UNITS) if i >= SLOTS}
FILLS = {u: i // SLOTS for i, u in enumerate(UNITS)}

CONST = {"ident": 128, "rows4": 128, "bias_sel": 24 * 32, "upper": 128, "strict": 128, "ones": 256,
         "inv": 512, "iota": 64, "thr": 3, "mask": 384}
C_AT, C_W = {}, 0
for _n, _w in CONST.items():
    C_AT[_n] = C_W
    C_W += _w
C_EARLY = C_AT["upper"]
PARAM = {"c": 8, "mix_g": 8, "pool_scale": 2, "conv_b": 2, "conv_g": 2, "conv_beta": 2,
         "conv_w": 2 * TAPS, "b_f": 1}
P_AT, P_W = {}, 0
for _n, _w in PARAM.items():
    P_AT[_n] = P_W
    P_W += _w
MISC = {"wf": KD * HEADS, "sg_w": HEADS * P, "pool_w": 2 * P, "sg_g": BW, "sg_beta": BW, "sg_bias": 2 * T}
M_AT, M_W = {}, 0
for _n, _w in MISC.items():
    M_AT[_n] = M_W
    M_W += _w
OUT_BANK = [6, 7, 4, 5]


def decoder_layer(nc, a, out):
    with ExitStack() as ctx:
        def sb(name, shape, dt=F32):
            return ctx.enter_context(nc.sbuf_tensor(name, shape, dt))

        def sem(name):
            return ctx.enter_context(nc.semaphore(name))

        def carver(region, size):
            at = [0]

            def carve(*shape, parts=P):
                n = 1
                for d in shape:
                    n *= d
                flat = region[0:parts, at[0]:at[0] + n]
                at[0] += n
                assert at[0] <= size, (at[0], size)
                if len(shape) == 1:
                    return flat
                names = "abcd"[:len(shape)]
                pattern = "p (" + " ".join(names) + ") -> p " + " ".join(names)
                return flat.rearrange(pattern, **{x: d for x, d in zip(names, shape)})
            return carve

        ring = sb("ring", [P, SLOTS, UNIT])
        const_misc = sb("const_misc", [P, C_W + M_W])
        const, misc = const_misc[:, 0:C_W], const_misc[:, C_W:C_W + M_W]
        shared_w2 = const_misc[:, C_W + M_W - UNIT:]
        par = sb("par", [P, P_W])
        x_sb = sb("x_sb", [P, TB, D])
        hT = sb("hT", [P, KD, T])
        router = sb("router", [P, KD, E])
        r_bias = sb("r_bias", [P, E])
        crep = sb("crep", [P, KD, 32])
        csig = sb("csig", [P, KD])
        cact = sb("cact", [P, KD])
        ada_b = sb("ada_b", [P, 256])
        part2 = sb("part2", [P, 2, 512])
        a_c = sb("a_c", [P, KD])
        s_c = sb("s_c", [P, KD])
        ssq = sb("ssq", [P, 8])
        rstd = sb("rstd", [P, 16])
        nmax = sb("nmax", [P, HEADS, 2])
        psum_p = sb("psum_p", [P, HEADS, 2])
        rden = sb("rden", [P, HEADS, 2])
        stats = sb("stats", [P, TB, 6])
        mv = sb("mv", [P, TB, 2])
        need = sb("need", [P, TB])
        wsum = sb("wsum", [P, TB])
        most = sb("most", [P, 1])
        over = sb("over", [P, 3])
        n_pass = sb("n_pass", [P, 1], I32)
        top8 = sb("top8", [P, TB, 8])

        def mi(name, pattern, **kw):
            return misc[:, M_AT[name]:M_AT[name] + MISC[name]].rearrange(pattern, **kw)

        wf = mi("wf", "p (k h) -> p k h", h=HEADS)
        sgw = mi("sg_w", "p (h t) -> p h t", h=HEADS)
        sg_g = misc[:, M_AT["sg_g"]:M_AT["sg_g"] + BW]
        sg_beta = misc[:, M_AT["sg_beta"]:M_AT["sg_beta"] + BW]
        sg_bias = mi("sg_bias", "p (j t) -> p j t", j=2)
        pool_w = mi("pool_w", "p (j d) -> p j d", j=2)

        PAD = TAPS - 1
        PP = 16
        KA = HD + 2
        reg1 = sb("reg1", [P, 2 * D])
        xn = reg1[:, :].rearrange("p (b d) -> p b d", b=TB)
        qa = reg1[0:KA, 0:D].rearrange("p (h t) -> p h t", h=HEADS)
        ka = reg1[0:KA, D:2 * D].rearrange("p (h t) -> p h t", h=HEADS)
        merged = reg1[:, :].rearrange("p (k t) -> p k t", k=KD)
        reg2 = sb("reg2", [P, 2 * D])
        part = reg2[:, :].rearrange("p (v d) -> p v d", v=2)
        probT = reg2[:, 0:HEADS * 384].rearrange("p (h t) -> p h t", h=HEADS)
        h2 = reg2[:, :].rearrange("p (b d) -> p b d", b=TB)
        reg3 = sb("reg3", [P, 2 * D])
        c3 = carver(reg3, 2 * D)
        zv, tv, zu, tu = c3(TB, BW), c3(TB, BW), c3(2, T), c3(2, T)
        gate_m, scale_f = reg3[:, 0:D], reg3[:, D:2 * D]
        final_g = scale_f
        reg4 = sb("reg4", [P, 2 * D])
        prob = reg4[:, 0:HEADS * 384].rearrange("p (h t) -> p h t", h=HEADS)
        gate_f, shift_f = reg4[:, 0:D], reg4[:, D:2 * D]
        W5 = 5 * (PP + T)
        reg5 = sb("reg5", [P, W5])
        junk = reg5[:, 0:D]
        c5 = carver(reg5, W5)
        w2s, w4s, w8s = c5(2, PP + T), c5(2, PP + T), c5(PP + T)
        W6 = 8284
        reg6 = sb("reg6", [P, W6])
        c6 = carver(reg6, W6)
        y = c6(NB, 2, T)
        gb = c6(2 * T)
        glu = c6(2, PAD + T)
        conv = c6(2, T)
        sq_c = c6(2, T)
        sig_c = c6(2, T)
        mean_c, rs_c = sig_c[:, 0, :], sig_c[:, 1, :]
        zp = c6(2, PP + T)
        pooled = c6(2, T)
        sig = c6(LAG + 2, 2 * T)
        logit = sig[:, 0:2, 0:384]
        v_sb = sig[:, 2, :].rearrange("p (b c) -> p b c", b=TB)
        fz = sig[0:HEADS, 3:5, :].rearrange("p a t -> p (a t)")[:, 0:3 * T].rearrange("p (r t) -> p r t", r=3)
        c6 = carver(reg6, W6)
        c6(NB * 2 * T + 2 * T)
        take = c6(TB * P).bitcast(BF16).rearrange("p (b t s) -> p b t s", b=2, t=TB)
        xg = c6(2, KD, P)
        turned = c6(2, 2, P)
        give = c6(TB * P).bitcast(BF16).rearrange("p (b t s) -> p b t s", b=2, t=TB)
        y_parts = c6(3 * D // 2).bitcast(BF16).rearrange("p (i d) -> p i d", i=3)
        y_rest = [c6(512)]
        ident_b = c6(P // 2).bitcast(BF16)
        gate_parts = c6(TB * 3 * E // 2).bitcast(BF16).rearrange("p (t i e) -> p t i e", t=TB, i=3)
        gate_pair = c6(2 * TB * 3).bitcast(BF16).rearrange("p (b t i e) -> p b t i e", b=2, t=TB, i=3)
        slot_gate = c6(2)
        c5 = carver(reg5, W5)
        sg1, th, hid = c5(FF), c5(FF), c5(FF)
        y_rest.append(c5(512))
        c6 = carver(reg6, NB * 2 * T)
        score, sel, gt = c6(TB, E), c6(TB, E), c6(TB, E)
        eq, pre, picked = c6(TB, E), c6(TB, E), c6(TB, E)
        top = c6(TB, GROUPS, 8)
        gs, gt_g, eq_g, pre_g = (c6(TB, GROUPS) for _ in range(4))
        pos = c6(TB, E)
        gates = c6(TB, E)
        gates_rest = c6(TB, E)
        hid_s = c6(TB, FF)
        parts = [r.bitcast(BF16).rearrange("p (b d) -> p b d", b=TB)
                 for r in (reg3[:, 0:D], reg4[:, D:2 * D], part2[:, :, :].rearrange("p m n -> p (m n)"))]
        hidT_s = gb.rearrange("p (b j t) -> p b j t", b=TB, j=2)

        bank = [ctx.enter_context(nc.psum_tensor(f"bank{i}", [P, 512], F32)) for i in range(8)]
        B_UNIT = [0, 1]
        B_ADA, B_CAST = 2, 3
        B_OUT = [0, 1, 2, 3]
        B_GATH, B_HID, B_Y = 4, 5, [6, 7]

        landed = [sem(f"landed{s}") for s in range(SLOTS)]
        w13_landed = [sem(f"w13_landed{r}") for r in range(RING_PAIRS)]
        w2_landed = [sem(f"w2_landed{r}") for r in range(RING_PAIRS)]
        w13_used = [sem(f"w13_used{r}") for r in range(RING_PAIRS)]
        w2_used = [sem(f"w2_used{r}") for r in range(RING_PAIRS)]
        names = """x_in const_in par_in ada_b_in misc_in late_in v_step a_step p_step
            final_in c_sig c_rep x_sq x_var x_rstd xn_done xT_done ada_done ada_read vec_done ac_done h_done
            unit_done f_done f_read exp_f cum_done cum_rows  conv_done
            q_done k_done tv_done sigv_done v_var v_rstd vn_done tu_done sigu_done
            sgw_done sg_done sg_y pooled_done pool_mm pool_y zero_done
            csum_done conv_c cvar_done conv_var conv_rstd conv_n conv_sig conv_y
            logits_done logit_done exp_done prob_done pT_done pT_read av_done av_y
            gb_done merged_done branch_done part2_done cast_done cast_read out_mm
            x2_done x2_sq x2_var x2_rstd h2_done h2T_done h2T_read
            part_done rest_done sc_mm score_done picked_done rank_done npass_done sh_done sh_sig sh_hid sh_T sh_TT sw2_in
            take_built pair_gates gate_mm slot_gated gathered gath_read sig1_done th_done hid_done turn_done turn_read
            give_read y0_done y_top y_less_top y_mid y_split pos_next sum_done ident_b_done x3_done x3_sq x3_var x3_rstd fin_done stored""".split()
        S = {n: sem(n) for n in names}
        unit_read = [sem(f"unit_read{b}") for b in range(2)]

        def cn(name, lo=0, hi=None):
            at = C_AT[name]
            return const[:, at + lo:at + (CONST[name] if hi is None else hi)]

        def pr(name, lo=0, hi=None):
            at = P_AT[name]
            return par[:, at + lo:at + (PARAM[name] if hi is None else hi)]

        ident = cn("ident")

        def unit(u):
            return ring[:, SLOT[u], :]

        def linker(eng, s):
            count = [0]

            def link(ins):
                count[0] += 1
                ins.then_inc(s, 1)
                eng.wait_ge(s, count[0])
            return link

        def source(u):
            kind, i = u
            if kind == "ada":
                return a["ada_w"][0, :, i * 256:(i + 1) * 256].rearrange("(p k) n -> p k n", k=KD)
            if kind in ("mix", "gate"):
                c = COL[MIX[i]] if kind == "mix" else COL["gate"] + (i % 4) * D + (i // 4) * 256
                return a["w_in"][0, :, c:c + 256].rearrange("(p k) n -> p k n", k=KD)
            if kind == "branch":
                return a["w_branch"][0, :, :, i * 256:(i + 1) * 256].rearrange("n (j p) d -> p (n j) d", p=P)
            if kind == "out":
                return a["w_out"][0, i * 256:(i + 1) * 256, :].rearrange("(j p) d -> p j d", p=P)
            return a["shared_" + kind[1:]][0].rearrange("(p k) f -> p (k f)", k=KD)

        def used_up(u):
            kind, i = u
            return {"ada": (S["ada_done"], i + 1), "mix": (S["unit_done"], i + 1), "gate": (S["unit_done"], 9 + i),
                    "branch": (S["branch_done"], 4 * i + 4), "out": (S["out_mm"], 4), "sw1": (S["sh_done"], TB),
                    "sw3": (S["sh_done"], TB)}[kind]

        w13_src = [a[n][0].rearrange("e (p k) f -> e p (k f)", k=KD) for n in ("exp_w1", "exp_w3")]
        w2_src = a["exp_w2"][0].rearrange("e (p j) d -> e p (j d)", j=2)

        block = ctx.enter_context(nc.Block())

        @block.sync
        def _(sp):
            sp.dma_start(x_sb[:, :, :], a["x"][0].rearrange("(b p) d -> p b d", p=P)).then_inc(S["x_in"], 16)
            for u in UNITS:
                if u in BEFORE:
                    sp.wait_ge(*used_up(BEFORE[u]))
                src = source(u)
                dst = unit(u)
                if len(src.shape) == 3:
                    dst = dst.rearrange("p (k n) -> p k n", k=src.shape[1])
                sp.dma_start(dst, src).then_inc(landed[SLOT[u]], 16)

            def load_13(r, e, w, it):
                sp.dma_start(ring[:, 6 * r + 2 * e + w, :],
                             w13_src[w][bass.ds(it * (2 * RING_PAIRS) + (2 * r + e), 1)].rearrange("e p n -> (e p) n"))\
                  .then_inc(w13_landed[r], 16)

            def load_2(r, e, it):
                sp.dma_start(ring[:, 6 * r + 4 + e, :],
                             w2_src[bass.ds(it * (2 * RING_PAIRS) + (2 * r + e), 1)].rearrange("e p n -> (e p) n"))\
                  .then_inc(w2_landed[r], 16)

            def load_step(use, it):
                for r in range(RING_PAIRS):
                    sp.wait_ge(w13_used[r], use)
                    for e in range(2):
                        for w in range(2):
                            load_13(r, e, w, it)
                    sp.wait_ge(w2_used[r], use)
                    for e in range(2):
                        load_2(r, e, it)

            for r in range(RING_PAIRS):
                for e in range(2):
                    for w in range(2):
                        sp.wait_ge(*used_up(LAST[6 * r + 2 * e + w]))
                        load_13(r, e, w, 0)
                for e in range(2):
                    sp.wait_ge(*used_up(LAST[6 * r + 4 + e]))
                    load_2(r, e, 0)
            with sp.Fori(1, STEPS - 1) as it:
                load_step(it, it)
            sp.wait_ge(S["npass_done"], 1)
            passes = sp.value_load(n_pass[0:1, 0:1], min_val=1, max_val=MAX_PASS)
            with sp.Fori(STEPS - 1, passes * STEPS) as use:
                load_step(use, use % STEPS)
            for k in range(4):
                sp.wait_ge(S["fin_done"], k + 1)
                tb, hf = k // 2, k % 2
                sp.dma_start(out[0, tb * P:(tb + 1) * P, hf * 512:(hf + 1) * 512],
                             h2[:, tb, hf * 512:(hf + 1) * 512]).then_inc(S["stored"], 16)
            sp.wait_ge(S["stored"], 64)

        @block.gpsimd
        def _(pool):
            link = linker(pool, S["p_step"])
            pool.wait_ge(S["ada_done"], 4)
            pool.dma_start(misc, a["misc"]).then_inc(S["misc_in"], 16)
            pool.dma_start(const[:, C_EARLY:], a["const"][:, C_EARLY:]).then_inc(S["misc_in"], 16)
            pool.dma_start(router[:, :, :], a["router_w"][0].rearrange("(p k) e -> p k e", k=KD)).then_inc(S["late_in"], 16)
            pool.dma_start(r_bias[:, :], a["router_bias"][0:1, :].partition_broadcast(P)).then_inc(S["late_in"], 16)
            link(pool.memset(glu[:, :, 0:PAD], 0.0))

            def fill(t, value, count):
                pool.memset(t, value).then_inc(S["zero_done"], 1)
                pool.wait_ge(S["zero_done"], count)

            fill(zp[:, :, 0:PP], 0.0, 1)
            pool.wait_ge(S["x_rstd"], 1)
            fill(w2s[:, :, 0:PP], 0.0, 2)
            fill(w4s[:, :, 0:PP], 0.0, 3)
            fill(w8s[:, 0:PP], 0.0, 4)
            pool.wait_ge(S["xT_done"], 2 * KD)
            fill(qa[HD:KA, :, :], 1.0, 5)
            fill(ka[HD:KA, :, :], 1.0, 6)
            pool.wait_ge(S["sg_y"], 1)
            pool.wait_ge(S["pool_mm"], 1)
            pool.dma_start(shared_w2, a["shared_w2"][0].rearrange("(p j) d -> p (j d)", j=2)).then_inc(S["sw2_in"], 16)
            pool.dma_start(scale_f, a["ffn_norm_g"][0:1, :].partition_broadcast(P)).then_inc(S["late_in"], 16)
            pool.wait_ge(S["h2_done"], TB)
            pool.dma_start(final_g, a["final_norm_g"].rearrange("(o d) -> o d", o=1).partition_broadcast(P))\
                .then_inc(S["final_in"], 16)
            pool.wait_ge(S["h2T_done"], 4)
            for i in range(2):
                pool.wait_ge(S["part_done"], i + 1)
                pool.tensor_tensor(h2, h2, parts[i], ALU.subtract).then_inc(S["rest_done"], 1)

        @block.scalar
        def _(act):
            link = linker(act, S["a_step"])
            act.dma_start(par[:, :], a["par"]).then_inc(S["par_in"], 16)
            act.dma_start(const[:, 0:C_EARLY], a["const"][:, 0:C_EARLY]).then_inc(S["const_in"], 16)
            act.dma_start(ada_b[:, :], a["ada_bp"]).then_inc(S["ada_b_in"], 16)
            act.wait_ge(S["par_in"], 16)
            act.activation(csig[:, :], pr("c"), ACT.Sigmoid).then_inc(S["c_sig"], 1)
            act.wait_ge(S["x_in"], 16)
            for tb in range(TB):
                link(act.activation(junk[:, :], x_sb[:, tb, :], ACT.Square, accum_out=ssq[:, tb:tb + 1]))
            act.activation(ssq[:, 2:4], ssq[:, 0:2], ACT.Copy, scale=1.0 / D).then_inc(S["x_sq"], 1)
            act.wait_ge(S["x_var"], 1)
            act.activation(rstd[:, 2:4], rstd[:, 0:2], ACT.Sqrt).then_inc(S["x_rstd"], 1)
            for b in range(4):
                act.wait_ge(S["ada_done"], 2 * b + 2)
                act.activation(part[:, b // 2, (b % 2) * 512:(b % 2 + 1) * 512], bank[b][:, :], ACT.Copy)\
                   .then_inc(S["ada_read"], 1)
            act.wait_ge(S["xT_done"], 2 * KD)
            act.wait_ge(S["ac_done"], 2)
            for k in range(4, KD):
                act.activation(hT[:, k, :], bank[4 + k // 2][:, (k % 2) * 256:(k % 2 + 1) * 256], ACT.Identity,
                               bias=s_c[:, k:k + 1], scale=a_c[:, k:k + 1]).then_inc(S["h_done"], 1)

            def read_unit(i):
                act.wait_ge(S["unit_done"], i + 1)

            def ub(i):
                return bank[B_UNIT[i % 2]]

            read_unit(0)
            act.activation(sig_c[:, :, :].rearrange("p j t -> p (j t)"), ub(0)[:, :], ACT.Sigmoid)\
               .then_inc(unit_read[0], 1)
            read_unit(2)
            act.wait_ge(S["zero_done"], 6)
            for h in range(HEADS):
                lo = 64 * (h % 2)
                ins = act.activation(qa[0:HD, h, :], ub(2)[lo:lo + HD, (h // 2) * T:(h // 2 + 1) * T], ACT.Copy,
                                     scale=HD ** -0.5)
                ins.then_inc(unit_read[0] if h == HEADS - 1 else S["q_done"], 1)
            act.wait_ge(S["f_read"], 2)
            link(act.activation(fz[:, 2, :], fz[:, 1, :], ACT.Exp, scale=-1.0))
            act.activation(fz[:, 1, :], fz[:, 2, :], ACT.Ln, bias=1.0).then_inc(S["exp_f"], 1)
            read_unit(3)
            for h in range(HEADS):
                lo = 64 * (h % 2)
                ins = act.activation(ka[0:HD, h, :], ub(3)[lo:lo + HD, (h // 2) * T:(h // 2 + 1) * T], ACT.Copy)
                ins.then_inc(unit_read[1] if h == HEADS - 1 else S["k_done"], 1)
            act.wait_ge(S["cum_done"], 2)
            act.dma_start(qa[HD:HD + 1, :, :], fz[:, 0:1, :]).then_inc(S["cum_rows"], 16)
            act.dma_start(ka[HD + 1:HD + 2, :, :], fz[:, 1:2, :]).then_inc(S["cum_rows"], 16)
            read_unit(4)
            act.activation(v_sb[:, :, :].rearrange("p b c -> p (b c)"), ub(4)[:, :], ACT.Copy)\
               .then_inc(unit_read[0], 1)

            def exps(h):
                act.wait_ge(S["logit_done"], 3 * (h + 1))
                for qb in range(2):
                    lo, n = (0, P) if qb == 0 else (P, T)
                    act.activation(prob[:, h, lo:lo + n], logit[:, h % 2, lo:lo + n], ACT.Exp,
                                   bias=nmax[:, h, qb:qb + 1], accum_out=psum_p[:, h, qb:qb + 1])\
                       .then_inc(S["exp_done"], 1)

            def probs_turned(h):
                act.wait_ge(S["pT_done"], h + 1)
                act.activation(probT[:, h, :], bank[4 + h][:, 0:384], ACT.Copy).then_inc(S["pT_read"], 1)

            exps(0)
            exps(1)
            read_unit(5)
            act.activation(zv[:, :, :].rearrange("p b c -> p (b c)"), ub(5)[:, :], ACT.Copy)\
               .then_inc(unit_read[1], 1)
            exps(2)
            exps(3)
            read_unit(6)
            act.activation(zu[:, :, :].rearrange("p b c -> p (b c)"), ub(6)[:, :], ACT.Copy)\
               .then_inc(unit_read[0], 1)
            probs_turned(0)
            probs_turned(1)
            read_unit(7)
            act.activation(zp[:, :, PP:PP + T], ub(7)[:, :].rearrange("p (j t) -> p j t", j=2), ACT.Copy)\
               .then_inc(unit_read[1], 1)
            act.wait_ge(S["tv_done"], 1)
            act.activation(tv[:, :, :], tv[:, :, :], ACT.Sigmoid).then_inc(S["sigv_done"], 1)
            act.wait_ge(S["tu_done"], 1)
            act.activation(tu[:, :, :], tu[:, :, :], ACT.Sigmoid).then_inc(S["sigu_done"], 1)
            probs_turned(2)
            probs_turned(3)
            act.wait_ge(S["v_var"], 1)
            act.activation(rstd[:, 14:16], rstd[:, 12:14], ACT.Sqrt).then_inc(S["v_rstd"], 1)
            act.wait_ge(S["av_done"], 1)
            act.activation(y[:, 3, :, :].rearrange("p j t -> p (j t)"), bank[4][:, :], ACT.Copy).then_inc(S["av_y"], 1)

            def cast_out(m):
                act.wait_ge(S["cast_done"], m + 1)
                if m == 0:
                    act.wait_ge(S["sg_y"], 1)
                which, cols = m // 2, slice((m % 2) * 512, (m % 2 + 1) * 512)
                if which != 2:
                    act.activation([gate_m, shift_f, None, gate_f][which][:, cols], bank[B_CAST][:, :], ACT.Copy)\
                       .then_inc(S["cast_read"], 1)

            for g in range(N_GATE):
                read_unit(8 + g)
                if g >= LAG + 2:
                    act.wait_ge(S["gb_done"], g - LAG - 1)
                act.activation(sig[:, g % (LAG + 2), :], ub(g)[:, :], ACT.Sigmoid).then_inc(unit_read[g % 2], 1)
                if g % 2 == 0 and g:
                    cast_out(g // 2 - 1)
                if g % 2:
                    m = g // 2
                    act.wait_ge(S["ada_done"], 8 + g + 1)
                    if m >= 2:
                        act.wait_ge(S["cast_done"], m - 1)
                    act.activation(part2[:, m % 2, :], bank[B_ADA][:, :], ACT.Copy).then_inc(S["part2_done"], 1)
                if g == CONV_AT:
                    act.wait_ge(S["conv_var"], 1)
                    act.activation(mean_c[:, :], rs_c[:, :], ACT.Sqrt).then_inc(S["conv_rstd"], 1)
                    act.wait_ge(S["conv_n"], 2)
                    act.activation(sq_c[:, :, :], conv[:, :, :], ACT.Sigmoid).then_inc(S["conv_sig"], 1)
            cast_out(7)
            for tb in range(TB):
                for k in (2 * tb, 2 * tb + 1):
                    cols = slice((k % 2) * 512, (k % 2 + 1) * 512)
                    act.wait_ge(S["x2_done"], k + 1)
                    act.activation(junk[:, cols], x_sb[:, tb, cols], ACT.Square, accum_out=ssq[:, 4 + k:5 + k])\
                       .then_inc(S["x2_sq"], 1)
                act.wait_ge(S["x2_var"], tb + 1)
                act.activation(rstd[:, 6 + tb:7 + tb], rstd[:, 4 + tb:5 + tb], ACT.Sqrt).then_inc(S["x2_rstd"], 1)
            for tb in range(TB):
                for q in range(2):
                    act.wait_ge(S["h2T_done"], 2 * tb + q + 1)
                    act.activation(hT[:, 4 * q:4 * q + 4, tb * P:(tb + 1) * P],
                                   bank[OUT_BANK[2 * tb + q]][:, :].rearrange("p (k t) -> p k t", k=4), ACT.Copy)\
                       .then_inc(S["h2T_read"], 1)

            def h_part(i):
                act.activation(parts[i], h2, ACT.Copy).then_inc(S["part_done"], 1)

            h_part(0)
            act.wait_ge(S["sc_mm"], 1)
            act.activation(score[:, :, :].rearrange("p b e -> p (b e)"), bank[4][:, 0:TB * E], ACT.Sigmoid)\
               .then_inc(S["score_done"], 1)
            act.wait_ge(S["rest_done"], 1)
            h_part(1)

            def shared_sigmoid(tb):
                act.wait_ge(S["sh_done"], tb + 1)
                act.activation(hid_s[:, tb, :], bank[5 + tb][:, 0:FF], ACT.Sigmoid).then_inc(S["sh_sig"], 1)

            shared_sigmoid(0)
            act.wait_ge(S["rest_done"], 2)
            h_part(2)
            shared_sigmoid(1)
            for q in range(2):
                act.wait_ge(S["gathered"], q + 1)
                act.activation(xg[:, 0, 4 * q:4 * q + 4, :].rearrange("p k s -> p (k s)"),
                               bank[B_GATH if q == 0 else B_Y[1]][:, :], ACT.Copy).then_inc(S["gath_read"], 1)

            def step(use):
                for r in range(RING_PAIRS):
                    n = use * RING_PAIRS + r
                    nxt = (r + 1) % 2

                    def copy_gathered(q):
                        act.wait_ge(S["gathered"], 2 * n + (3 + q))
                        act.activation(xg[:, nxt, 4 * q:4 * q + 4, :].rearrange("p k s -> p (k s)"),
                                       bank[B_GATH][:, :], ACT.Copy).then_inc(S["gath_read"], 1)

                    copy_gathered(0)
                    act.wait_ge(w13_used[r], use + 1)
                    act.activation(sg1[:, :], bank[B_HID][:, 0:FF], ACT.Sigmoid).then_inc(S["sig1_done"], 1)
                    copy_gathered(1)
                    act.wait_ge(S["turn_done"], n + 1)
                    act.activation(turned[:, r, :, :].rearrange("p k s -> p (k s)"), bank[B_HID][:, 0:2 * P], ACT.Copy)\
                       .then_inc(S["turn_read"], 1)
                    act.activation(give[:, r, :, :].rearrange("p t s -> p (t s)"), bank[B_HID][:, 2 * P:4 * P], ACT.Copy)\
                       .then_inc(S["give_read"], 1)
                    act.wait_ge(S["y0_done"], n + 1)
                    act.activation(y_parts[:, 0, 0:512], bank[B_Y[0]][:, :], ACT.Copy).then_inc(S["y_top"], 1)
                    act.wait_ge(w2_used[r], use + 1)
                    act.activation(y_parts[:, 0, 512:D], bank[B_Y[1]][:, :], ACT.Copy).then_inc(S["y_top"], 1)
                    for hf in range(2):
                        act.wait_ge(S["y_less_top"], 2 * n + (hf + 1))
                        act.activation(y_parts[:, 1, hf * 512:(hf + 1) * 512], y_rest[hf], ACT.Copy)\
                           .then_inc(S["y_mid"], 1)

            with act.Fori(0, SPLIT) as use:
                step(use)
            act.wait_ge(S["sh_T"], 1)
            act.activation(hidT_s[:, :, :, :].rearrange("p b j t -> p (b j t)"), bank[B_GATH][:, :], ACT.Copy)\
               .then_inc(S["sh_TT"], 1)
            act.wait_ge(S["npass_done"], 1)
            passes = act.value_load(n_pass[0:1, 0:1], min_val=1, max_val=MAX_PASS)
            with act.Fori(SPLIT, passes * STEPS) as use:
                step(use)
            for tb in range(TB):
                for k in (2 * tb, 2 * tb + 1):
                    cols = slice((k % 2) * 512, (k % 2 + 1) * 512)
                    act.wait_ge(S["x3_done"], k + 1)
                    act.activation(junk[:, cols], x_sb[:, tb, cols], ACT.Square, accum_out=ssq[:, k:k + 1])\
                       .then_inc(S["x3_sq"], 1)
                act.wait_ge(S["x3_var"], tb + 1)
                act.activation(rstd[:, 10 + tb:11 + tb], rstd[:, 8 + tb:9 + tb], ACT.Sqrt).then_inc(S["x3_rstd"], 1)

        @block.vector
        def _(dve):
            link = linker(dve, S["v_step"])
            dve.wait_ge(S["x_sq"], 1)
            link(dve.tensor_scalar(rstd[:, 0:2], ssq[:, 2:4], EPS, None, ALU.add))
            dve.reciprocal(rstd[:, 0:2], rstd[:, 0:2]).then_inc(S["x_var"], 1)
            dve.wait_ge(S["c_sig"], 1)
            link(dve.tensor_tensor(cact[:, :], csig[:, :], pr("c"), ALU.mult))
            dve.tensor_copy(crep[:, :, :], cact[:, :].unsqueeze(2).to_broadcast([P, KD, 32])).then_inc(S["c_rep"], 1)
            dve.wait_ge(S["x_rstd"], 1)
            for tb in range(TB):
                dve.tensor_scalar(xn[:, tb, :], x_sb[:, tb, :], rstd[:, 2 + tb:3 + tb], None, ALU.mult)\
                   .then_inc(S["xn_done"], 1)
            dve.wait_ge(S["vec_done"], 1)
            dve.scalar_tensor_tensor(out=a_c[:, :], in0=bank[0][:, KD:2 * KD], scalar=1.0, in1=pr("mix_g"),
                                     op0=ALU.add, op1=ALU.mult).then_inc(S["ac_done"], 1)
            dve.tensor_copy(s_c[:, :], bank[0][:, 0:KD]).then_inc(S["ac_done"], 1)
            dve.wait_ge(S["ac_done"], 2)
            dve.wait_ge(S["xT_done"], 2 * KD)
            for k in range(4):
                dve.tensor_scalar(hT[:, k, :], bank[4 + k // 2][:, (k % 2) * 256:(k % 2 + 1) * 256], a_c[:, k:k + 1],
                                  s_c[:, k:k + 1], ALU.mult, ALU.add).then_inc(S["h_done"], 1)
            dve.wait_ge(S["misc_in"], 32)
            for h in range(HEADS):
                dve.tensor_tensor(sgw[:, h, :], sgw[:, h, :], cn("upper"), ALU.mult).then_inc(S["sgw_done"], 1)
            dve.wait_ge(S["unit_done"], 2)
            dve.wait_ge(unit_read[0], 1)
            dve.wait_ge(S["p_step"], 1)
            dve.tensor_tensor(glu[:, :, PAD:PAD + T], bank[1][:, :].rearrange("p (j t) -> p j t", j=2),
                              sig_c[:, :, :], ALU.mult).then_inc(unit_read[1], 1)
            dve.wait_ge(S["f_done"], 1)
            dve.tensor_scalar(fz[:, 0, :], bank[7][0:HEADS, 0:T], par[0:HEADS, P_AT["b_f"]:P_AT["b_f"] + 1], None,
                              ALU.add).then_inc(S["f_read"], 1)
            dve.wait_ge(S["f_read"], 1)
            dve.scalar_tensor_tensor(out=fz[:, 1, :], in0=fz[:, 0, :], scalar=-1.0, in1=fz[:, 0, :],
                                     op0=ALU.mult, op1=ALU.max).then_inc(S["f_read"], 1)
            dve.wait_ge(S["exp_f"], 1)
            link(dve.scalar_tensor_tensor(out=fz[:, 2, :], in0=fz[:, 0, :], scalar=0.0, in1=fz[:, 1, :],
                                          op0=ALU.min, op1=ALU.subtract))
            dve.tensor_tensor_scan(fz[:, 0, :], const[0:HEADS, C_AT["ones"]:C_AT["ones"] + T], fz[:, 2, :], 0.0,
                                   ALU.mult, ALU.add).then_inc(S["cum_done"], 1)
            dve.wait_ge(S["cum_done"], 1)
            dve.tensor_scalar(fz[:, 1, :], fz[:, 0, :], -1.0, None, ALU.mult).then_inc(S["cum_done"], 1)

            dve.wait_ge(unit_read[1], 1)
            for i in range(TAPS):
                for j in range(2):
                    w = pr("conv_w", j * TAPS + i, j * TAPS + i + 1)
                    src = glu[:, j, i:i + T]
                    if i:
                        dve.wait_ge(S["conv_done"], 2 * i + j - 1)
                        ins = dve.scalar_tensor_tensor(out=conv[:, j, :], in0=src, scalar=w, in1=conv[:, j, :],
                                                       op0=ALU.mult, op1=ALU.add)
                    else:
                        ins = dve.tensor_scalar(conv[:, j, :], src, w, pr("conv_b", j, j + 1), ALU.mult, ALU.add)
                    ins.then_inc(S["conv_done"], 1)

            def mask_and_max(h):
                dve.wait_ge(S["logits_done"], h + 1)
                if h >= 2:
                    dve.wait_ge(S["exp_done"], 2 * (h - 1))
                dve.tensor_tensor(logit[:, h % 2, :], bank[4 + h][:, 0:384], cn("mask"), ALU.add)\
                   .then_inc(S["logit_done"], 1)
                dve.wait_ge(S["logit_done"], 3 * h + 1)
                for qb in range(2):
                    lo, n = (0, P) if qb == 0 else (P, T)
                    dve.tensor_reduce(nmax[:, h, qb:qb + 1], logit[:, h % 2, lo:lo + n], AX, ALU.max, negate=True)\
                       .then_inc(S["logit_done"], 1)

            def normalise(h):
                dve.wait_ge(S["exp_done"], 2 * (h + 1))
                link(dve.reciprocal(rden[:, h, :], psum_p[:, h, :]))
                for qb in range(2):
                    lo, n = (0, P) if qb == 0 else (P, T)
                    dve.tensor_scalar(prob[:, h, lo:lo + n], prob[:, h, lo:lo + n], rden[:, h, qb:qb + 1], None, ALU.mult)\
                       .then_inc(S["prob_done"], 1)

            mask_and_max(0)
            mask_and_max(1)
            normalise(0)
            normalise(1)
            mask_and_max(2)
            mask_and_max(3)
            normalise(2)
            normalise(3)

            def gelu_inner(t, z):
                link(dve.tensor_tensor(t, z, z, ALU.mult))
                link(dve.tensor_scalar(t, t, 1.5957691216057308 * 0.044715, 1.5957691216057308, ALU.mult, ALU.add))
                return dve.tensor_tensor(t, t, z, ALU.mult)

            dve.wait_ge(unit_read[1], 3)
            gelu_inner(tv[:, :, :], zv[:, :, :]).then_inc(S["tv_done"], 1)
            dve.wait_ge(unit_read[0], 4)
            gelu_inner(tu[:, :, :], zu[:, :, :]).then_inc(S["tu_done"], 1)
            dve.wait_ge(S["sigv_done"], 1)
            link(dve.tensor_tensor(zv[:, :, :], zv[:, :, :], tv[:, :, :], ALU.mult))
            for tb in range(TB):
                link(dve.bn_stats(stats[:, tb, :], zv[:, tb, :]))
                link(dve.bn_aggr(mv[:, tb, :], stats[:, tb, :]))
            link(dve.tensor_scalar(rstd[:, 12:14], mv[:, :, 1], EPS, None, ALU.add))
            dve.reciprocal(rstd[:, 12:14], rstd[:, 12:14]).then_inc(S["v_var"], 1)
            dve.wait_ge(unit_read[1], 4)
            dve.wait_ge(S["zero_done"], 6)
            link(dve.tensor_tensor(w2s[:, :, 1:], zp[:, :, 1:], zp[:, :, 0:PP + T - 1], ALU.add))
            link(dve.tensor_tensor(w4s[:, :, 2:], w2s[:, :, 2:], w2s[:, :, 0:PP + T - 2], ALU.add))
            link(dve.tensor_tensor(w8s[:, 4:], w4s[:, 1, 4:], w4s[:, 1, 0:PP + T - 4], ALU.add))
            inv = cn("inv").rearrange("p (j t) -> p j t", j=2)
            link(dve.tensor_tensor(pooled[0:64, 0, :], w2s[0:64, 0, PP:], inv[0:64, 0, :], ALU.mult))
            link(dve.tensor_tensor(pooled[64:P, 0, :], w4s[64:P, 0, PP:], inv[64:P, 0, :], ALU.mult))
            link(dve.tensor_tensor(pooled[0:64, 1, :], w8s[0:64, PP:], inv[0:64, 1, :], ALU.mult))
            link(dve.tensor_tensor(pooled[64:P, 1, :], w8s[64:P, PP:], w8s[64:P, PP - 8:PP + T - 8], ALU.add))
            link(dve.tensor_tensor(pooled[64:P, 1, :], pooled[64:P, 1, :], inv[64:P, 1, :], ALU.mult))
            dve.tensor_tensor(pooled[:, :, :], pooled[:, :, :], zp[:, :, PP:], ALU.subtract).then_inc(S["pooled_done"], 1)
            dve.wait_ge(S["v_rstd"], 1)
            for tb in range(TB):
                link(dve.tensor_scalar(zv[:, tb, :], zv[:, tb, :], mv[:, tb, 0:1], rstd[:, 14 + tb:15 + tb],
                                       ALU.subtract, ALU.mult))
                link(dve.tensor_tensor(zv[:, tb, :], zv[:, tb, :], sg_g[:, :], ALU.mult))
                dve.tensor_tensor(zv[:, tb, :], zv[:, tb, :], sg_beta[:, :], ALU.add).then_inc(S["vn_done"], 1)
            dve.wait_ge(S["sigu_done"], 1)
            link(dve.tensor_tensor(zu[:, :, :], zu[:, :, :], tu[:, :, :], ALU.mult))
            dve.wait_ge(S["sg_done"], 1)
            link(dve.tensor_tensor(tu[:, :, :], bank[5][:, :].rearrange("p (j t) -> p j t", j=2), sg_bias[:, :, :], ALU.add))
            dve.tensor_tensor(y[:, 1, :, :], tu[:, :, :], zu[:, :, :], ALU.mult).then_inc(S["sg_y"], 1)
            dve.wait_ge(S["pool_mm"], 1)
            for j in range(2):
                dve.tensor_scalar(y[:, 0, j, :], bank[6][:, j * T:(j + 1) * T], pr("pool_scale", j, j + 1), None, ALU.mult)\
                   .then_inc(S["pool_y"], 1)

            def conv_norm_1():
                dve.wait_ge(S["csum_done"], 1)
                link(dve.tensor_scalar(mean_c[:, :], bank[7][:, 0:T], 1.0 / BW, None, ALU.mult))
                for j in range(2):
                    link(dve.tensor_tensor(conv[:, j, :], conv[:, j, :], mean_c[:, :], ALU.subtract))
                dve.tensor_tensor(sq_c[:, :, :], conv[:, :, :], conv[:, :, :], ALU.mult).then_inc(S["conv_c"], 1)

            def conv_norm_2():
                dve.wait_ge(S["cvar_done"], 1)
                link(dve.tensor_scalar(rs_c[:, :], bank[6][:, 0:T], 1.0 / BW, EPS, ALU.mult, ALU.add))
                dve.reciprocal(rs_c[:, :], rs_c[:, :]).then_inc(S["conv_var"], 1)

            def merge(g):
                dc, n = g // 4, g % 4
                dve.wait_ge(S["branch_done"], g + 1)
                dst = merged[:, 2 * dc:2 * dc + 2, :].rearrange("p k t -> p (k t)")
                o = dst if n == 0 else gb[:, :]
                if n and 3 * dc + n > 1:
                    dve.wait_ge(S["merged_done"], 3 * dc + n - 1)
                dve.tensor_tensor(o, bank[4 + g % 2][:, :], sig[:, g % (LAG + 2), :], ALU.mult).then_inc(S["gb_done"], 1)
                if n:
                    dve.wait_ge(S["gb_done"], g + 1)
                    dve.tensor_tensor(dst, dst, gb[:, :], ALU.add).then_inc(S["merged_done"], 1)

            def scale_rows(hf):
                cols = slice(hf * 512, (hf + 1) * 512)
                dve.wait_ge(S["cast_done"], 5 + hf)
                dve.wait_ge(S["late_in"], 48)
                dve.scalar_tensor_tensor(out=scale_f[:, cols], in0=bank[B_CAST][:, :], scalar=1.0, in1=scale_f[:, cols],
                                         op0=ALU.add, op1=ALU.mult).then_inc(S["cast_read"], 1)

            conv_norm_1()
            conv_norm_2()
            dve.wait_ge(S["conv_rstd"], 1)
            for j in range(2):
                link(dve.tensor_tensor(conv[:, j, :], conv[:, j, :], mean_c[:, :], ALU.mult))
                dve.tensor_scalar(conv[:, j, :], conv[:, j, :], pr("conv_g", j, j + 1), pr("conv_beta", j, j + 1),
                                  ALU.mult, ALU.add).then_inc(S["conv_n"], 1)
            dve.wait_ge(S["conv_sig"], 1)
            dve.tensor_tensor(y[:, 2, :, :], conv[:, :, :], sq_c[:, :, :], ALU.mult).then_inc(S["conv_y"], 1)
            for g in range(N_GATE):
                merge(g)
                if g == 10 - LAG:
                    scale_rows(0)
                if g == 12 - LAG:
                    scale_rows(1)
            for tb in range(TB):
                for k in (2 * tb, 2 * tb + 1):
                    cols = slice((k % 2) * 512, (k % 2 + 1) * 512)
                    dve.wait_ge(S["out_mm"], k + 1)
                    if k == 0:
                        dve.wait_ge(S["cast_read"], 2)
                    if k:
                        dve.wait_ge(S["x2_done"], k)
                    link(dve.tensor_tensor(gb[:, :], bank[OUT_BANK[k]][:, :], gate_m[:, cols], ALU.mult))
                    dve.tensor_tensor(x_sb[:, tb, cols], x_sb[:, tb, cols], gb[:, :], ALU.add).then_inc(S["x2_done"], 1)
                dve.wait_ge(S["x2_sq"], 2 * tb + 2)
                link(dve.tensor_tensor(rstd[:, 4 + tb:5 + tb], ssq[:, 4 + 2 * tb:5 + 2 * tb],
                                       ssq[:, 5 + 2 * tb:6 + 2 * tb], ALU.add))
                link(dve.tensor_scalar(rstd[:, 4 + tb:5 + tb], rstd[:, 4 + tb:5 + tb], 1.0 / D, EPS, ALU.mult, ALU.add))
                dve.reciprocal(rstd[:, 4 + tb:5 + tb], rstd[:, 4 + tb:5 + tb]).then_inc(S["x2_var"], 1)
                dve.wait_ge(S["x2_rstd"], tb + 1)
                link(dve.scalar_tensor_tensor(out=h2[:, tb, :], in0=x_sb[:, tb, :], scalar=rstd[:, 6 + tb:7 + tb],
                                              in1=scale_f[:, :], op0=ALU.mult, op1=ALU.mult))
                dve.tensor_tensor(h2[:, tb, :], h2[:, tb, :], shift_f[:, :], ALU.add).then_inc(S["h2_done"], 1)

            def pick(vals, n, k, m_gt, m_eq, m_pre):
                for tb in range(TB):
                    link(dve.max(top8[:, tb, :], vals[:, tb, :]))
                kth = top8[:, :, k - 1:k].to_broadcast([P, TB, n])
                link(dve.tensor_tensor(m_gt, vals, kth, ALU.is_gt))
                link(dve.tensor_tensor(m_eq, vals, kth, ALU.is_equal))
                link(dve.tensor_reduce(need[:, :], m_gt, AX, ALU.add))
                link(dve.tensor_scalar(need[:, :], need[:, :], -1.0, float(k), ALU.mult, ALU.add))
                for tb in range(TB):
                    link(dve.tensor_tensor_scan(m_pre[:, tb, :], cn("ones", 0, n), m_eq[:, tb, :], 0.0, ALU.mult, ALU.add))
                link(dve.tensor_tensor(m_pre, m_pre, need[:, :].unsqueeze(2).to_broadcast([P, TB, n]), ALU.is_le))
                link(dve.tensor_tensor(m_eq, m_eq, m_pre, ALU.mult))
                return dve.tensor_tensor(m_gt, m_gt, m_eq, ALU.add)

            dve.memset(give[:, 1, :, :], 0.0).then_inc(S["give_read"], 1)
            dve.memset(y_parts[:, :, :], 0.0).then_inc(S["y_split"], 2)
            dve.tensor_copy(ident_b, ident).then_inc(S["ident_b_done"], 1)
            dve.wait_ge(S["score_done"], 1)
            link(dve.tensor_tensor(sel[:, :, :], score[:, :, :], r_bias[:, :].unsqueeze(1).to_broadcast([P, TB, E]), ALU.add))
            for tb in range(TB):
                for g in range(GROUPS):
                    ins = dve.max(top[:, tb, g, :], sel[:, tb, 8 * g:8 * g + 8])
            link(ins)
            link(dve.tensor_tensor(gs[:, :, :], top[:, :, :, 0], top[:, :, :, 1], ALU.add))
            link(pick(gs[:, :, :], GROUPS, TOPG, gt_g[:, :, :], eq_g[:, :, :], pre_g[:, :, :]))
            link(dve.tensor_scalar(gt_g[:, :, :], gt_g[:, :, :], -NEG, NEG, ALU.mult, ALU.add))
            link(dve.tensor_tensor(sel[:, :, :].rearrange("p b (g i) -> p (b g) i", g=GROUPS),
                                   sel[:, :, :].rearrange("p b (g i) -> p (b g) i", g=GROUPS),
                                   gt_g[:, :, :].rearrange("p b g -> p (b g)").unsqueeze(2).to_broadcast([P, TB * GROUPS, 8]),
                                   ALU.add))
            pick(sel[:, :, :], E, TOPK, picked[:, :, :], eq[:, :, :], pre[:, :, :]).then_inc(S["picked_done"], 1)
            dve.wait_ge(S["picked_done"], 1)
            dve.wait_ge(S["rank_done"], 1)
            link(dve.scalar_tensor_tensor(out=pos[:, :, 0:E], in0=bank[4][:, 0:TB * E].rearrange("p (b e) -> p b e", b=TB),
                                          scalar=1.0, in1=picked[:, :, :], op0=ALU.add, op1=ALU.mult))
            link(dve.tensor_scalar(pos[:, :, 0:E], pos[:, :, 0:E], -1.0, None, ALU.add))
            link(dve.tensor_reduce(most[:, :], bank[4][:, TB * E:(TB + 1) * E], AX, ALU.max))
            link(dve.tensor_tensor(over[:, :], most[:, 0:1].to_broadcast([P, 3]), cn("thr"), ALU.is_gt))
            link(dve.tensor_reduce(most[:, :], over[:, :], AX, ALU.add))
            dve.tensor_scalar(n_pass[:, :], most[:, :], 1.0, None, ALU.add).then_inc(S["npass_done"], 1)

            iota = cn("iota").unsqueeze(1).to_broadcast([P, 2, CAP])

            def build(b, first, before):
                sl = slice(first, first + 2) if isinstance(first, int) else bass.ds(first, 2)
                if not isinstance(first, int):
                    dve.wait_ge(S["pos_next"], before)
                for tb in range(TB):
                    pp = pos[:, tb, sl].unsqueeze(2).to_broadcast([P, 2, CAP])
                    dve.tensor_tensor(take[:, b, tb, :].rearrange("p (e s) -> p e s", e=2), iota, pp, ALU.is_equal)\
                       .then_inc(S["take_built"], 1)
                dve.wait_ge(S["take_built"], before * 2 + 2)
                dve.tensor_scalar(pos[:, :, sl], pos[:, :, sl], -float(CAP), None, ALU.add).then_inc(S["pos_next"], 1)

            def pair_gates(b, first):
                sl = slice(first, first + 2) if isinstance(first, int) else bass.ds(first, 2)
                dve.tensor_copy(gate_pair[:, b, :, :, :].rearrange("p t i e -> p (t i) e"),
                                gate_parts[:, :, :, sl].rearrange("p t i e -> p (t i) e")).then_inc(S["pair_gates"], 1)

            build(0, 0, 0)
            build(1, 2, 1)
            link(dve.tensor_tensor(gt[:, :, :], score[:, :, :], picked[:, :, :], ALU.mult))
            link(dve.tensor_reduce(wsum[:, :], gt[:, :, :], AX, ALU.add))
            link(dve.reciprocal(wsum[:, :], wsum[:, :]))
            link(dve.tensor_scalar(wsum[:, :], wsum[:, :], ROUTE_SCALE, None, ALU.mult))
            link(dve.tensor_tensor(gates[:, :, 0:E], gt[:, :, :], wsum[:, :].unsqueeze(2).to_broadcast([P, TB, E]), ALU.mult))
            link(dve.tensor_copy(gate_parts[:, :, 0, :], gates[:, :, :]))
            link(dve.tensor_tensor(gates_rest[:, :, :], gates[:, :, :], gate_parts[:, :, 0, :], ALU.subtract))
            link(dve.tensor_copy(gate_parts[:, :, 1, :], gates_rest[:, :, :]))
            link(dve.tensor_tensor(gate_parts[:, :, 2, :], gates_rest[:, :, :], gate_parts[:, :, 1, :], ALU.subtract))
            pair_gates(0, 0)
            pair_gates(1, 2)
            for tb in range(TB):
                dve.wait_ge(S["sh_sig"], tb + 1)
                link(dve.tensor_tensor(hid_s[:, tb, :], hid_s[:, tb, :], bank[5 + tb][:, 0:FF], ALU.mult))
                dve.tensor_tensor(hid_s[:, tb, :], hid_s[:, tb, :], bank[5 + tb][:, FF:2 * FF], ALU.mult)\
                   .then_inc(S["sh_hid"], 1)
            def step(use):
                for r in range(RING_PAIRS):
                    n = use * RING_PAIRS + r
                    dve.wait_ge(S["sig1_done"], n + 1)
                    dve.tensor_tensor(th[:, :], sg1[:, :], bank[B_HID][:, 0:FF], ALU.mult).then_inc(S["th_done"], 1)
                    dve.wait_ge(S["th_done"], n + 1)
                    dve.wait_ge(S["gate_mm"], n + 1)
                    dve.tensor_copy(slot_gate[:, r:r + 1], bank[B_Y[0]][:, 0:1]).then_inc(S["slot_gated"], 1)
                    dve.wait_ge(S["slot_gated"], n + 1)
                    dve.scalar_tensor_tensor(out=hid[:, :], in0=th[:, :], scalar=slot_gate[:, r:r + 1],
                                             in1=bank[B_HID][:, FF:2 * FF], op0=ALU.mult, op1=ALU.mult)\
                       .then_inc(S["hid_done"], 1)
                    dve.wait_ge(S["turn_done"], n + 1)
                    first = (use + 1) % STEPS * (2 * RING_PAIRS) + 2 * r
                    build(r, first, n + 2)
                    pair_gates(r, first)
                    for hf in range(2):
                        cols = slice(hf * 512, (hf + 1) * 512)
                        dve.wait_ge(S["y_top"], 2 * n + (hf + 1))
                        dve.tensor_tensor(y_rest[hf], bank[B_Y[hf]][:, :], y_parts[:, 0, cols], ALU.subtract)\
                           .then_inc(S["y_less_top"], 1)
                    for hf in range(2):
                        cols = slice(hf * 512, (hf + 1) * 512)
                        dve.wait_ge(S["y_mid"], 2 * n + (hf + 1))
                        dve.tensor_tensor(y_parts[:, 2, cols], y_rest[hf], y_parts[:, 1, cols], ALU.subtract)\
                           .then_inc(S["y_split"], 1)

            with dve.Fori(0, SPLIT) as use:
                step(use)
            dve.wait_ge(S["npass_done"], 1)
            passes = dve.value_load(n_pass[0:1, 0:1], min_val=1, max_val=MAX_PASS)
            with dve.Fori(SPLIT, passes * STEPS) as use:
                step(use)
            dve.wait_ge(S["final_in"], 16)
            for tb in range(TB):
                for k in (2 * tb, 2 * tb + 1):
                    cols = slice((k % 2) * 512, (k % 2 + 1) * 512)
                    dve.wait_ge(S["sum_done"], k + 1)
                    if k == 0:
                        dve.wait_ge(S["cast_read"], 8)
                    if k:
                        dve.wait_ge(S["x3_done"], k)
                    link(dve.tensor_tensor(gb[:, :], bank[B_OUT[k]][:, :], gate_f[:, cols], ALU.mult))
                    dve.tensor_tensor(x_sb[:, tb, cols], x_sb[:, tb, cols], gb[:, :], ALU.add).then_inc(S["x3_done"], 1)
                dve.wait_ge(S["x3_sq"], 2 * tb + 2)
                link(dve.tensor_tensor(rstd[:, 8 + tb:9 + tb], ssq[:, 2 * tb:1 + 2 * tb], ssq[:, 1 + 2 * tb:2 + 2 * tb], ALU.add))
                link(dve.tensor_scalar(rstd[:, 8 + tb:9 + tb], rstd[:, 8 + tb:9 + tb], 1.0 / D, EPS, ALU.mult, ALU.add))
                dve.reciprocal(rstd[:, 8 + tb:9 + tb], rstd[:, 8 + tb:9 + tb]).then_inc(S["x3_var"], 1)
                dve.wait_ge(S["x3_rstd"], tb + 1)
                for hf in range(2):
                    cols = slice(hf * 512, (hf + 1) * 512)
                    dve.scalar_tensor_tensor(out=h2[:, tb, cols], in0=x_sb[:, tb, cols], scalar=rstd[:, 10 + tb:11 + tb],
                                             in1=final_g[:, cols], op0=ALU.mult, op1=ALU.mult).then_inc(S["fin_done"], 1)

        @block.tensor
        def _(pe):
            def mm(o, lhsT, rhs, start=True, stop=True):
                return pe.matmul(o, lhsT, rhs, start=start, stop=stop, skip_group_check=True)

            def ready(u):
                pe.wait_ge(landed[SLOT[u]], 16 * (FILLS[u] + 1))

            pe.wait_ge(S["const_in"], 16)

            def ada(i, b):
                u = ("ada", i)
                ready(u)
                w = unit(u).rearrange("p (k n) -> p k n", k=KD)
                cols = slice((i % 2) * 256, (i % 2 + 1) * 256)
                for k in range(KD):
                    q = 32 * (k % 4)
                    mm(bank[b][q:q + 32, cols], crep[:, k, :], w[:, k, :], start=k < 4, stop=k >= 5)
                sel_row = cn("bias_sel", i * 32, (i + 1) * 32)
                mm(bank[b][0:32, cols], sel_row, ada_b[:, :], start=False, stop=True).then_inc(S["ada_done"], 1)
            pe.wait_ge(S["c_rep"], 1)
            pe.wait_ge(S["ada_b_in"], 16)
            for i in range(3):
                ada(i, i // 2)
            for tb in range(TB):
                pe.wait_ge(S["xn_done"], tb + 1)
                for k in range(KD):
                    pe.transpose(bank[4 + k // 2][:, (k % 2) * T + tb * P:(k % 2) * T + (tb + 1) * P],
                                 xn[:, tb, k::KD],
                                 ident).then_inc(S["xT_done"], 1)
            for i in range(3, 8):
                ada(i, i // 2)
            pe.wait_ge(S["ada_read"], 4)
            for v in range(2):
                for k in range(KD):
                    ins = mm(bank[0][:, v * KD + k:v * KD + k + 1], part[:, v, k::KD], cn("rows4", 0, 1))
            ins.then_inc(S["vec_done"], 1)

            def begin_unit(i, u):
                ready(u)
                if i >= 2:
                    pe.wait_ge(unit_read[i % 2], i // 2)
                return bank[B_UNIT[i % 2]], unit(u).rearrange("p (k n) -> p k n", k=KD)

            def channels(i, u):
                b, w = begin_unit(i, u)
                for m in range(2):
                    for k in range(KD):
                        ins = mm(b[:, m * T:(m + 1) * T], w[:, k, m * P:(m + 1) * P], hT[:, k, :], k == 0, k == KD - 1)
                ins.then_inc(S["unit_done"], 1)

            def tokens(i, u):
                b, w = begin_unit(i, u)
                for tb in range(TB):
                    for k in range(KD):
                        ins = mm(b[:, tb * BW:(tb + 1) * BW], hT[:, k, tb * P:(tb + 1) * P], w[:, k, :], k == 0, k == KD - 1)
                ins.then_inc(S["unit_done"], 1)

            def logits(h):
                b = bank[4 + h]
                mm(b[:, 0:P], qa[:, h, 0:P], ka[:, h, 0:P])
                mm(b[:, P:P + T], qa[:, h, P:T], ka[:, h, :]).then_inc(S["logits_done"], 1)

            def turn_probs(h):
                pe.wait_ge(S["prob_done"], 2 * h + 2)
                for q in range(3):
                    ins = pe.transpose(bank[4 + h][:, q * P:(q + 1) * P], prob[:, h, q * P:(q + 1) * P], ident)
                ins.then_inc(S["pT_done"], 1)

            pe.wait_ge(S["h_done"], 8)
            channels(0, ("mix", 0))
            channels(1, ("mix", 1))
            channels(2, ("mix", 2))
            pe.wait_ge(S["misc_in"], 32)
            for k in range(KD):
                ins = mm(bank[7][0:HEADS, 0:T], wf[:, k, :], hT[:, k, :], k == 0, k == KD - 1)
            ins.then_inc(S["f_done"], 1)
            channels(3, ("mix", 3))
            tokens(4, ("mix", 4))
            pe.wait_ge(unit_read[0], 2)
            pe.wait_ge(unit_read[1], 2)
            pe.wait_ge(S["cum_rows"], 32)
            for h in range(HEADS):
                logits(h)
            tokens(5, ("mix", 5))
            channels(6, ("mix", 6))
            turn_probs(0)
            turn_probs(1)
            channels(7, ("mix", 7))
            turn_probs(2)
            turn_probs(3)

            def attend():
                pe.wait_ge(unit_read[0], 3)
                for h in range(HEADS):
                    pe.wait_ge(S["pT_read"], HEADS if h == 0 else h + 1)
                    lo, c = 64 * (h % 2), (h // 2) * T
                    vh = slice(h * HD, (h + 1) * HD)
                    mm(bank[4][lo:lo + HD, c:c + P], v_sb[:, 0, vh], probT[:, h, 0:P])
                    mm(bank[4][lo:lo + HD, c + P:c + T], v_sb[:, 0, vh], probT[:, h, P:T], True, False)
                    ins = mm(bank[4][lo:lo + HD, c + P:c + T], v_sb[:, 1, vh], probT[:, h, T:T + P], False, True)
                ins.then_inc(S["av_done"], 1)

            def spatial():
                pe.wait_ge(S["vn_done"], TB)
                pe.wait_ge(S["sgw_done"], HEADS)
                for h in range(HEADS):
                    lo, c = 64 * (h % 2), (h // 2) * T
                    for tb in range(TB):
                        ins = mm(bank[5][lo:lo + HD, c + tb * P:c + (tb + 1) * P], zv[:, tb, h * HD:(h + 1) * HD],
                                 sgw[:, h, :])
                ins.then_inc(S["sg_done"], 1)

            def pool_linear():
                pe.wait_ge(S["pooled_done"], 1)
                for j in range(2):
                    ins = mm(bank[6][:, j * T:(j + 1) * T], pool_w[:, j, :], pooled[:, j, :])
                ins.then_inc(S["pool_mm"], 1)

            def channel_sum(b, src, done):
                for j in range(2):
                    ins = mm(b[:, 0:T], cn("ones", 0, P), src[:, j, :], j == 0, j == 1)
                ins.then_inc(done, 1)

            def cast(m):
                pe.wait_ge(S["part2_done"], m + 1)
                if m:
                    pe.wait_ge(S["cast_read"], m)
                mm(bank[B_CAST][:, :], cn("rows4"), part2[:, m % 2, :]).then_inc(S["cast_done"], 1)

            def branch(g):
                dc, n = g // 4, g % 4
                b = bank[4 + g % 2]
                if n == 0:
                    ready(("branch", dc))
                if g < 4:
                    pe.wait_ge(*[(S["pool_y"], 2), (S["sg_y"], 1), (S["conv_y"], 1), (S["av_y"], 1)][n])
                if g == 0:
                    pe.wait_ge(S["av_y"], 1)
                if g >= 2:
                    pe.wait_ge(S["gb_done"], g - 1)
                w = unit(("branch", dc)).rearrange("p (n j d) -> p n j d", n=NB, j=2)
                for m in range(2):
                    for j in range(2):
                        ins = mm(b[:, m * T:(m + 1) * T], w[:, n, j, m * P:(m + 1) * P], y[:, n, j, :], j == 0, j == 1)
                ins.then_inc(S["branch_done"], 1)

            for g in range(N_GATE):
                channels(8 + g, ("gate", g))
                if g == 0:
                    attend()
                if g == 1:
                    spatial()
                    pool_linear()
                if g == CONV_AT - 1:
                    pe.wait_ge(S["conv_done"], 2 * TAPS)
                    channel_sum(bank[7], conv, S["csum_done"])
                if g == CONV_AT:
                    pe.wait_ge(S["conv_c"], 1)
                    pe.wait_ge(S["pool_y"], 2)
                    channel_sum(bank[6], sq_c, S["cvar_done"])
                if g % 2 == 0 and g:
                    cast(g // 2 - 1)
                if g % 2 == 0 and g:
                    pe.wait_ge(S["part2_done"], g // 2)
                ada(8 + g, B_ADA)
                if g >= LAG:
                    branch(g - LAG)
            cast(7)
            for g in range(N_GATE - LAG, N_GATE):
                branch(g)

            for i in range(4):
                ready(("out", i))
            for k in range(4):
                tb, hf = k // 2, k % 2
                if k == 0:
                    pe.wait_ge(S["conv_var"], 1)
                    pe.wait_ge(S["conv_c"], 1)
                if k == 2:
                    pe.wait_ge(S["gb_done"], N_GATE)
                for j in range(KD):
                    pe.wait_ge(S["merged_done"], 3 * (j // 2 + 1))
                    w = unit(("out", j // 2))
                    ins = mm(bank[OUT_BANK[k]][:, :], merged[:, j, tb * P:(tb + 1) * P],
                             w[:, (j % 2) * D + hf * 512:(j % 2) * D + (hf + 1) * 512], j == 0, j == KD - 1)
                ins.then_inc(S["out_mm"], 1)

            for tb in range(TB):
                pe.wait_ge(S["h2_done"], tb + 1)
                for q in range(2):
                    for k in range(4):
                        ins = pe.transpose(bank[OUT_BANK[2 * tb + q]][:, k * P:(k + 1) * P],
                                           h2[:, tb, 4 * q + k::KD], ident)
                    ins.then_inc(S["h2T_done"], 1)

            pe.wait_ge(S["h2T_read"], 4)
            pe.wait_ge(S["late_in"], 48)
            for tb in range(TB):
                for k in range(KD):
                    ins = mm(bank[4][:, tb * E:(tb + 1) * E], hT[:, k, tb * P:(tb + 1) * P], router[:, k, :],
                             k == 0, k == KD - 1)
            ins.then_inc(S["sc_mm"], 1)
            for u in (("sw1", 0), ("sw3", 0)):
                ready(u)
            lo = SLOT[("sw1", 0)]
            sw13 = ring[:, lo:lo + 2, :].rearrange("p w (k f) -> p w k f", k=KD)

            def shared_hidden(tb):
                for k in range(KD):
                    ins = mm(bank[5 + tb][:, :].rearrange("p (w f) -> p w f", w=2), hT[:, k, tb * P:(tb + 1) * P],
                             sw13[:, :, k, :], k == 0, k == KD - 1)
                ins.then_inc(S["sh_done"], 1)

            shared_hidden(0)
            pe.wait_ge(S["picked_done"], 1)
            mm(bank[4][:, 0:E], cn("strict"), picked[:, 0, :])
            mm(bank[4][:, E:2 * E], cn("ones", 0, P), picked[:, 0, :], True, False)
            mm(bank[4][:, E:2 * E], cn("strict"), picked[:, 1, :], False, True)
            mm(bank[4][:, 2 * E:3 * E], cn("ones", 0, P), picked[:, 0, :], True, False)
            mm(bank[4][:, 2 * E:3 * E], cn("ones", 0, P), picked[:, 1, :], False, True).then_inc(S["rank_done"], 1)
            shared_hidden(1)

            def gather(b, q, to=B_GATH):
                for k in range(4):
                    for tb in range(TB):
                        for i in range(3):
                            ins = mm(bank[to][:, k * P:(k + 1) * P], parts[i][:, tb, 4 * q + k::KD],
                                     take[:, b, tb, :], tb == 0 and i == 0, tb == 1 and i == 2)
                ins.then_inc(S["gathered"], 1)

            pe.wait_ge(S["npass_done"], 1)
            pe.wait_ge(S["take_built"], 2)
            pe.wait_ge(S["part_done"], 3)
            gather(0, 0)
            gather(0, 1, B_Y[1])
            pe.wait_ge(S["give_read"], 1)
            pe.wait_ge(S["y_split"], 2)
            for k in range(4):
                mm(bank[B_OUT[k]][:, :], give[:, 1, 0, :], y_parts[:, 0, 0:512], True, False)
            pe.wait_ge(S["sh_hid"], TB)

            def scatter(b, k, stop=False):
                tb, hf = k // 2, k % 2
                for i in range(3):
                    ins = mm(bank[B_OUT[k]][:, :], give[:, b, tb, :], y_parts[:, i, hf * 512:(hf + 1) * 512],
                             False, stop and i == 2)
                return ins

            pe.wait_ge(S["ident_b_done"], 1)

            def step(use):
                for r in range(RING_PAIRS):
                    n = use * RING_PAIRS + r
                    nxt = (r + 1) % 2
                    pe.wait_ge(S["take_built"], 2 * n + 4)
                    pe.wait_ge(S["gath_read"], 2 * n + 2)
                    gather(nxt, 0)
                    pe.wait_ge(w13_landed[r], (use + 1) * 64)
                    pe.wait_ge(S["give_read"], n + 1)
                    w13 = ring[:, 6 * r:6 * r + 4, :].rearrange("p (e w) (k f) -> p e w k f", e=2, k=KD)
                    for k in range(KD):
                        for e in range(2):
                            q = CAP * e
                            ins = mm(bank[B_HID][q:q + CAP, :].rearrange("p (w f) -> p w f", w=2),
                                     xg[:, r, k, q:q + CAP], w13[:, e, :, k, :], k == 0, k == KD - 1)
                    ins.then_inc(w13_used[r], 1)
                    pe.wait_ge(S["y_split"], 2 * n + 2)
                    pe.wait_ge(S["pair_gates"], n + 1)
                    for e in range(2):
                        q = CAP * e
                        for tb in range(TB):
                            for i in range(3):
                                ins = mm(bank[B_Y[0]][q:q + CAP, 0:1], take[:, r, tb, q:q + CAP],
                                         gate_pair[:, r, tb, i, e:e + 1], tb == 0 and i == 0, tb == 1 and i == 2)
                    ins.then_inc(S["gate_mm"], 1)
                    pe.wait_ge(S["gath_read"], 2 * n + 3)
                    gather(nxt, 1)
                    scatter(nxt, 0)
                    scatter(nxt, 1)
                    pe.wait_ge(S["hid_done"], n + 1)
                    for tb in range(TB):
                        mm(bank[B_HID][:, (2 + tb) * P:(3 + tb) * P], take[:, r, tb, :], ident_b)
                    for j in range(2):
                        ins = pe.transpose(bank[B_HID][:, j * P:(j + 1) * P], hid[:, j::2], ident)
                    ins.then_inc(S["turn_done"], 1)
                    scatter(nxt, 2)
                    scatter(nxt, 3)
                    pe.wait_ge(S["turn_read"], n + 1)
                    pe.wait_ge(w2_landed[r], (use + 1) * 32)
                    for hf in range(2):
                        for j in range(2):
                            for e in range(2):
                                q = CAP * e
                                ins = mm(bank[B_Y[hf]][q:q + CAP, :], turned[:, r, j, q:q + CAP],
                                         ring[:, 6 * r + 4 + e, j * D + hf * 512:j * D + (hf + 1) * 512], j == 0, j == 1)
                        ins.then_inc(w2_used[r] if hf else S["y0_done"], 1)

            with pe.Fori(0, SPLIT) as use:
                step(use)
            pe.wait_ge(S["gath_read"], 2 * RING_PAIRS * SPLIT + 2)
            for tb in range(TB):
                for j in range(2):
                    ins = pe.transpose(bank[B_GATH][:, (2 * tb + j) * P:(2 * tb + j + 1) * P], hid_s[:, tb, j::2], ident)
            ins.then_inc(S["sh_T"], 1)
            pe.wait_ge(S["sw2_in"], 16)
            pe.wait_ge(S["sh_TT"], 1)
            for k in range(4):
                tb, hf = k // 2, k % 2
                for j in range(2):
                    mm(bank[B_OUT[k]][:, :], hidT_s[:, tb, j, :],
                       shared_w2[:, j * D + hf * 512:j * D + (hf + 1) * 512], False, False)
            passes = pe.value_load(n_pass[0:1, 0:1], min_val=1, max_val=MAX_PASS)
            with pe.Fori(SPLIT, passes * STEPS) as use:
                step(use)
            last = passes * (2 * PAIRS)
            pe.wait_ge(S["y_split"], last + 2)
            for k in range(4):
                scatter(1, k, True).then_inc(S["sum_done"], 1)


def constants():
    import numpy as np
    c = {n: np.zeros((P, w), np.float32) for n, w in CONST.items()}
    i, j = np.arange(P)[:, None], np.arange(P)[None, :]
    c["ident"][:] = i == j
    c["upper"][:] = i <= j
    c["strict"][:] = i < j
    c["ones"][:] = 1
    c["rows4"][0::32] = 1
    causal = np.where(j <= i, 0, NEG).astype(np.float32)
    c["mask"][:, 0:P] = causal
    c["mask"][:, 2 * P:3 * P] = causal
    t = np.arange(T) + 1
    for g in range(4):
        c["inv"][64 * (g % 2):64 * (g % 2) + 64, (g // 2) * T:(g // 2 + 1) * T] = 1.0 / np.minimum(t, 2 ** (g + 1))
    c["iota"][:] = np.arange(CAP)
    c["thr"][:] = [CAP, 2 * CAP, 3 * CAP]
    for u in range(24):
        c["bias_sel"][u, 32 * u:32 * u + 32] = 1
    return np.concatenate([c[n] for n in CONST], 1)


def lay_out(inp):
    import numpy as np
    cols = [inp["c"][0].reshape(P, KD), inp["mix_norm_g"][0].reshape(P, KD)]
    cols += [inp[n][0].reshape(2, P).T for n in ("pool_scale", "conv_b", "conv_ln_g", "conv_ln_b")]
    cols.append(inp["conv_w"][0].reshape(TAPS, 2, P).transpose(2, 1, 0).reshape(P, 2 * TAPS))
    b_f = np.zeros((P, 1), np.float32)
    b_f[0:HEADS, 0] = inp["b_f"][0]
    par = np.concatenate(cols + [b_f], 1)
    wf = inp["w_in"][0][:, COL["f"]:COL["f"] + HEADS].reshape(P, KD * HEADS)
    sg_w = inp["sg_w"][0].transpose(2, 0, 1).reshape(P, HEADS * P)
    pool_w = np.zeros((P, 2, P), np.float32)
    sg_bias = np.zeros((P, 2, TB, P), np.float32)
    for g in range(4):
        lo = 64 * (g % 2)
        pool_w[lo:lo + 64, g // 2, lo:lo + 64] = inp["pool_w"][0, g]
        sg_bias[lo:lo + 64, g // 2] = inp["sg_b"][0, g]
    rows = [np.repeat(inp[n], P, 0) for n in ("sg_ln_g", "sg_ln_b")]
    misc = np.concatenate([wf, sg_w, pool_w.reshape(P, -1)] + rows + [sg_bias.reshape(P, -1)], 1)
    ada_bp = np.zeros((P, 256), np.float32)
    ada_bp[0:24] = inp["ada_b"][0].reshape(24, 256)
    return par, misc, ada_bp


_INS = ["x", "w_in", "w_branch", "w_out", "ffn_norm_g", "ada_w", "router_w", "router_bias", "exp_w1", "exp_w3", "exp_w2",
        "shared_w1", "shared_w3", "shared_w2", "final_norm_g"]


def kernel(**inputs):
    import numpy as np
    import concourse.bacc as bacc
    from concourse.bass_utils import run_bass_kernel_spmd

    nc = bacc.Bacc("TRN2", target_bir_lowering=False, num_devices=1)
    arrays = {n: np.ascontiguousarray(inputs[n]) for n in _INS}
    small = {n: np.asarray(inputs[n]) for n in ("c", "mix_norm_g", "pool_scale", "conv_b", "conv_ln_g", "conv_ln_b", "conv_w",
                                                "b_f", "w_in", "sg_w", "pool_w", "sg_b", "sg_ln_g", "sg_ln_b", "ada_b")}
    arrays["par"], arrays["misc"], arrays["ada_bp"] = lay_out(small)
    arrays["const"] = constants()
    arrays = {n + "_dram": v for n, v in arrays.items()}
    aps = {n[:-5]: nc.dram_tensor(n, v.shape, mybir.dt.from_np(v.dtype), kind="ExternalInput").ap()
           for n, v in arrays.items()}
    out = nc.dram_tensor("out_dram", (1, T, D), F32, kind="ExternalOutput").ap()
    decoder_layer(nc, aps, out)
    r = run_bass_kernel_spmd(nc, [arrays], core_ids=[0])
    return r.results[0]["out_dram"]
```
